# Optimizing a Trainium2 kernel written in Bass

```python
import jax, jax.numpy as jnp
from jax import lax
import numpy as np
import math

D_MODEL = 1024
BATCH = 1
SEQ = 512
DEPTH = 4

N_MIXERS = 3
D_FF = 4 * D_MODEL
Q_BLOCK = 128
ROPE_BASE = 10000.0
EPS = 1e-6
NEG_INF = -1e30

MLA_HEADS = 8
MLA_Q_RANK = 256
MLA_KV_RANK = 128
MLA_NOPE = 128
MLA_ROPE = 64
MLA_V = 128

SB_HEADS = 16
SB_HEAD_DIM = D_MODEL // SB_HEADS

RET_HEADS = 4
RET_KEY_DIM = D_MODEL // RET_HEADS
RET_VAL_DIM = 2 * D_MODEL // RET_HEADS
RET_CHUNK = 128

N_MLA_LAYERS = (DEPTH + 2) // 3
N_SB_LAYERS = (DEPTH + 1) // 3
N_RET_LAYERS = DEPTH // 3


def rms_norm(x, g):
    xf = x.astype(jnp.float32)
    y = xf * lax.rsqrt(jnp.mean(xf * xf, axis=-1, keepdims=True) + EPS)
    return (y * g.astype(jnp.float32)).astype(x.dtype)

def modulate(x, shift, scale):
    return x * (1.0 + scale[:, None, :]) + shift[:, None, :]

def rope_tables(positions, dim):
    inv_freq = ROPE_BASE ** (-jnp.arange(0, dim, 2, dtype=jnp.float32) / dim)
    ang = positions.astype(jnp.float32)[..., None] * inv_freq
    return jnp.cos(ang)[:, :, None, :], jnp.sin(ang)[:, :, None, :]

def apply_rope(t, cos, sin):
    t1, t2 = jnp.split(t, 2, axis=-1)
    cos = cos.astype(t.dtype)
    sin = sin.astype(t.dtype)
    return jnp.concatenate([t1 * cos - t2 * sin, t2 * cos + t1 * sin], axis=-1)

def to_blocks(t, size):
    b, s, h, d = t.shape
    return t.reshape(b, s // size, size, h, d).transpose(1, 0, 2, 3, 4)

def from_blocks(t):
    nb, b, size, h, d = t.shape
    return t.transpose(1, 0, 2, 3, 4).reshape(b, nb * size, h, d)

def blocked_causal_softmax(q, k, v, scale):
    k_pos = jnp.arange(k.shape[1])
    qb = to_blocks(q, Q_BLOCK)

    def one_block(args):
        q_blk, b_idx = args
        q_pos = b_idx * Q_BLOCK + jnp.arange(Q_BLOCK)
        s = jnp.einsum('bqhd,bkhd->bhqk', q_blk, k).astype(jnp.float32) * scale
        s = jnp.where(k_pos[None, :] <= q_pos[:, None], s, NEG_INF)
        p = jax.nn.softmax(s, axis=-1).astype(v.dtype)
        return jnp.einsum('bhqk,bkhd->bqhd', p, v)

    o = lax.map(one_block, (qb, jnp.arange(qb.shape[0])))
    return from_blocks(o)

def mla_mixer(h, positions, w_in, q_norm, kv_norm, w_q_up, w_kv_up, w_out):
    b, s, _ = h.shape
    q_lat, kv_lat, k_pe = jnp.split(h @ w_in, [MLA_Q_RANK, MLA_Q_RANK + MLA_KV_RANK], axis=-1)
    cos, sin = rope_tables(positions, MLA_ROPE)
    q = (rms_norm(q_lat, q_norm) @ w_q_up).reshape(b, s, MLA_HEADS, MLA_NOPE + MLA_ROPE)
    q_nope, q_pe = jnp.split(q, [MLA_NOPE], axis=-1)
    q = jnp.concatenate([q_nope, apply_rope(q_pe, cos, sin)], axis=-1)
    kv = (rms_norm(kv_lat, kv_norm) @ w_kv_up).reshape(b, s, MLA_HEADS, MLA_NOPE + MLA_V)
    k_nope, v = jnp.split(kv, [MLA_NOPE], axis=-1)
    k_pe = apply_rope(k_pe[:, :, None, :], cos, sin)
    k = jnp.concatenate([k_nope, jnp.broadcast_to(k_pe, (b, s, MLA_HEADS, MLA_ROPE))], axis=-1)
    o = blocked_causal_softmax(q, k, v, (MLA_NOPE + MLA_ROPE) ** -0.5)
    return o.reshape(b, s, MLA_HEADS * MLA_V) @ w_out

def stick_breaking_mixer(h, w_in, w_out):
    b, s, _ = h.shape
    q, k, v = jnp.split(h @ w_in, 3, axis=-1)
    q = q.reshape(b, s, SB_HEADS, SB_HEAD_DIM)
    k = k.reshape(b, s, SB_HEADS, SB_HEAD_DIM)
    v = v.reshape(b, s, SB_HEADS, SB_HEAD_DIM)
    scale = SB_HEAD_DIM ** -0.5
    k_pos = jnp.arange(s)
    qb = to_blocks(q, Q_BLOCK)

    def one_block(args):
        q_blk, b_idx = args
        q_pos = b_idx * Q_BLOCK + jnp.arange(Q_BLOCK)
        z = jnp.einsum('bqhd,bkhd->bhqk', q_blk, k).astype(jnp.float32) * scale
        strict = k_pos[None, :] < q_pos[:, None]
        log_1m = jnp.where(strict, jax.nn.log_sigmoid(-z), 0.0)
        suffix = lax.cumsum(log_1m, axis=3, reverse=True) - log_1m
        a = jnp.where(strict, jnp.exp(jax.nn.log_sigmoid(z) + suffix), 0.0).astype(v.dtype)
        return jnp.einsum('bhqk,bkhd->bqhd', a, v)

    o = from_blocks(lax.map(one_block, (qb, jnp.arange(qb.shape[0]))))
    return o.reshape(b, s, SB_HEADS * SB_HEAD_DIM) @ w_out

def retention_mixer(h, positions, w_in, gn_g, w_out):
    b, s, _ = h.shape
    hk = RET_HEADS * RET_KEY_DIM
    hv = RET_HEADS * RET_VAL_DIM
    q, k, v, g = jnp.split(h @ w_in, [hk, 2 * hk, 2 * hk + hv], axis=-1)
    cos, sin = rope_tables(positions, RET_KEY_DIM)
    q = apply_rope(q.reshape(b, s, RET_HEADS, RET_KEY_DIM), cos, sin).astype(jnp.float32)
    k = apply_rope(k.reshape(b, s, RET_HEADS, RET_KEY_DIM), cos, sin).astype(jnp.float32) * (RET_KEY_DIM ** -0.5)
    v = v.reshape(b, s, RET_HEADS, RET_VAL_DIM).astype(jnp.float32)

    log_gamma = jnp.log(1.0 - 2.0 ** (-5.0 - jnp.arange(RET_HEADS, dtype=jnp.float32)))
    idx = jnp.arange(RET_CHUNK, dtype=jnp.float32)
    diff = idx[:, None] - idx[None, :]
    decay = jnp.where(diff[None] >= 0, jnp.exp(jnp.maximum(diff, 0.0)[None] * log_gamma[:, None, None]), 0.0)
    xi = jnp.exp((idx[:, None] + 1.0) * log_gamma[None, :])
    zeta = jnp.exp((RET_CHUNK - 1.0 - idx)[:, None] * log_gamma[None, :])
    g_chunk = jnp.exp(RET_CHUNK * log_gamma)

    def step(state, inp):
        qc, kc, vc = inp
        sc = jnp.einsum('bihd,bjhd->bhij', qc, kc) * decay[None]
        inner = jnp.einsum('bhij,bjhv->bihv', sc, vc)
        cross = jnp.einsum('bihd,bhdv->bihv', qc, state) * xi[None, :, :, None]
        state = state * g_chunk[None, :, None, None] + jnp.einsum('bjhd,bjhv->bhdv', kc * zeta[None, :, :, None], vc)
        return state, inner + cross

    state0 = jnp.zeros((b, RET_HEADS, RET_KEY_DIM, RET_VAL_DIM), jnp.float32)
    _, o = lax.scan(step, state0, (to_blocks(q, RET_CHUNK), to_blocks(k, RET_CHUNK), to_blocks(v, RET_CHUNK)))
    o = from_blocks(o)
    o = o * lax.rsqrt(jnp.mean(o * o, axis=-1, keepdims=True) + EPS)
    o = o.reshape(b, s, hv) * gn_g.astype(jnp.float32)
    o = (jax.nn.silu(g.astype(jnp.float32)) * o).astype(h.dtype)
    return o @ w_out

def first_inputs(seed: int = 0) -> dict:
    key = jax.random.key(seed)
    ks = jax.random.split(key, 24)

    def dense(k, shape, fan_in, gain=1.0):
        return jax.random.normal(k, shape, jnp.float32) * (gain * fan_in ** -0.5)

    def gains(k, shape):
        return 1.0 + 0.05 * jax.random.normal(k, shape, jnp.float32)

    hk = RET_HEADS * RET_KEY_DIM
    hv = RET_HEADS * RET_VAL_DIM
    return {
        "x": jax.random.normal(ks[0], (BATCH, SEQ, D_MODEL), jnp.float32),
        "c": jax.random.normal(ks[1], (BATCH, D_MODEL), jnp.float32),
        "positions": jnp.broadcast_to(jnp.arange(SEQ, dtype=jnp.int32), (BATCH, SEQ)),
        "ada_w": dense(ks[2], (DEPTH, D_MODEL, 6 * D_MODEL), D_MODEL, 0.5),
        "ada_b": 0.01 * jax.random.normal(ks[3], (DEPTH, 6 * D_MODEL), jnp.float32),
        "norm_g": gains(ks[4], (DEPTH, 4, D_MODEL)),
        "ffn_w1": dense(ks[5], (DEPTH, D_MODEL, D_FF), D_MODEL),
        "ffn_w2": dense(ks[6], (DEPTH, D_FF, D_MODEL), D_FF),
        "mla_w_in": dense(ks[7], (N_MLA_LAYERS, D_MODEL, MLA_Q_RANK + MLA_KV_RANK + MLA_ROPE), D_MODEL),
        "mla_q_norm": gains(ks[8], (N_MLA_LAYERS, MLA_Q_RANK)),
        "mla_kv_norm": gains(ks[9], (N_MLA_LAYERS, MLA_KV_RANK)),
        "mla_w_q_up": dense(ks[10], (N_MLA_LAYERS, MLA_Q_RANK, MLA_HEADS * (MLA_NOPE + MLA_ROPE)), MLA_Q_RANK),
        "mla_w_kv_up": dense(ks[11], (N_MLA_LAYERS, MLA_KV_RANK, MLA_HEADS * (MLA_NOPE + MLA_V)), MLA_KV_RANK),
        "mla_w_out": dense(ks[12], (N_MLA_LAYERS, MLA_HEADS * MLA_V, D_MODEL), MLA_HEADS * MLA_V),
        "sb_w_in": dense(ks[13], (N_SB_LAYERS, D_MODEL, 3 * SB_HEADS * SB_HEAD_DIM), D_MODEL),
        "sb_w_out": dense(ks[14], (N_SB_LAYERS, SB_HEADS * SB_HEAD_DIM, D_MODEL), SB_HEADS * SB_HEAD_DIM),
        "ret_w_in": dense(ks[15], (N_RET_LAYERS, D_MODEL, 2 * hk + 2 * hv), D_MODEL),
        "ret_gn_g": gains(ks[16], (N_RET_LAYERS, hv)),
        "ret_w_out": dense(ks[17], (N_RET_LAYERS, hv, D_MODEL), hv),
    }

def first_block(x, c, positions, ada_w, ada_b, norm_g, ffn_w1, ffn_w2,
              mla_w_in, mla_q_norm, mla_kv_norm, mla_w_q_up, mla_w_kv_up, mla_w_out,
              sb_w_in, sb_w_out, ret_w_in, ret_gn_g, ret_w_out):
    cond = jax.nn.silu(c)
    for i in range(DEPTH):
        mod = cond @ ada_w[i] + ada_b[i]
        sh_a, sc_a, g_a, sh_f, sc_f, g_f = jnp.split(mod, 6, axis=-1)

        h = modulate(rms_norm(x, norm_g[i, 0]), sh_a, sc_a)
        kind, j = i % N_MIXERS, i // N_MIXERS
        if kind == 0:
            y = mla_mixer(h, positions, mla_w_in[j], mla_q_norm[j], mla_kv_norm[j],
                          mla_w_q_up[j], mla_w_kv_up[j], mla_w_out[j])
        elif kind == 1:
            y = stick_breaking_mixer(h, sb_w_in[j], sb_w_out[j])
        else:
            y = retention_mixer(h, positions, ret_w_in[j], ret_gn_g[j], ret_w_out[j])
        x = x + g_a[:, None, :] * rms_norm(y, norm_g[i, 1])

        h = modulate(rms_norm(x, norm_g[i, 2]), sh_f, sc_f)
        y = jnp.square(jax.nn.relu(h @ ffn_w1[i])) @ ffn_w2[i]
        x = x + g_f[:, None, :] * rms_norm(y, norm_g[i, 3])
    return x


DEPTH_2 = 1

HEAD_DIM = 64
ROPE_DIMS = HEAD_DIM // 4
ROPE_THETA = 500000.0
NORM_EPS = 1e-6
NEG_INF_2 = -1e30

NSA_HEADS = 8
NSA_KV_GROUPS = 2
NSA_Q_PER_KV = NSA_HEADS // NSA_KV_GROUPS
CMP_BLOCK = 32
CMP_STRIDE = 16
CMP_HIDDEN = 256
SLC_BLOCK = 64
SLC_TOPN = 16
FORCE_SCORE = 1e3
WIN = 512
NSA_QBLOCK = 64

DIL_PATTERNS = ((128, 1), (512, 4), (2048, 16))
DIL_GROUPS = len(DIL_PATTERNS)
DIL_HEADS_PER_GROUP = 4
DIL_WIDTH = DIL_HEADS_PER_GROUP * HEAD_DIM
DIL_BLOCK = 128

NSA_Q_COLS = NSA_HEADS * HEAD_DIM
NSA_KV_COLS = NSA_KV_GROUPS * HEAD_DIM
NSA_GATE_COLS = 3 * NSA_HEADS
DIL_COLS = DIL_GROUPS * 3 * DIL_WIDTH
MERGE_COLS = 2 * D_MODEL
IN_COLS = NSA_Q_COLS + 6 * NSA_KV_COLS + NSA_GATE_COLS + DIL_COLS + MERGE_COLS

PEER_HEADS = 8
PEER_NKEYS = 128
PEER_TOPK = 16
PEER_QDIM = 128
PEER_N_EXPERTS = PEER_NKEYS ** 2
PEER_CHUNK = 128


def rms_norm_2(z, g):
    zf = z.astype(jnp.float32)
    zf = zf * lax.rsqrt(jnp.mean(zf * zf, axis=-1, keepdims=True) + NORM_EPS)
    return (zf * g.astype(jnp.float32)).astype(z.dtype)

def rope(z, pos):
    half = ROPE_DIMS // 2
    inv = ROPE_THETA ** (-(jnp.arange(half, dtype=jnp.float32) * 2.0 / ROPE_DIMS))
    ang = pos.astype(jnp.float32)[:, None] * inv[None, :]
    cos = jnp.cos(ang)[None, :, None, :]
    sin = jnp.sin(ang)[None, :, None, :]
    zf = z.astype(jnp.float32)
    z1 = zf[..., :half]
    z2 = zf[..., half:ROPE_DIMS]
    out = jnp.concatenate([z1 * cos - z2 * sin, z1 * sin + z2 * cos, zf[..., ROPE_DIMS:]], axis=-1)
    return out.astype(z.dtype)

def compress_blocks(z, idx, pe, w1, w2):
    B, _, G, dh = z.shape
    blk = z[:, idx] + pe[None, None, :, None, :]
    n_cmp = idx.shape[0]
    flat = blk.transpose(0, 1, 3, 2, 4).reshape(B, n_cmp, G, CMP_BLOCK * dh)
    return jax.nn.gelu(flat @ w1) @ w2

def nsa_attention(q, k_c, v_c, k_s, v_s, k_w, v_w, gate_logits, q_norm, k_norm,
                  cmp_pe_k, cmp_w1_k, cmp_w2_k, cmp_pe_v, cmp_w1_v, cmp_w2_v):
    B, S, _ = q.shape
    G, HG, dh = NSA_KV_GROUPS, NSA_Q_PER_KV, HEAD_DIM
    scale = HEAD_DIM ** -0.5
    dtype = q.dtype
    pos = jnp.arange(S, dtype=jnp.int32)
    q = rope(rms_norm_2(q.reshape(B, S, NSA_HEADS, dh), q_norm), pos)
    shp = (B, S, G, dh)
    k_s = rope(rms_norm_2(k_s.reshape(shp), k_norm[1]), pos)
    k_w = rope(rms_norm_2(k_w.reshape(shp), k_norm[2]), pos)
    v_s = v_s.reshape(shp)
    v_w = v_w.reshape(shp)

    n_cmp = (S - CMP_BLOCK) // CMP_STRIDE + 1
    starts = jnp.arange(n_cmp, dtype=jnp.int32) * CMP_STRIDE
    idx = starts[:, None] + jnp.arange(CMP_BLOCK, dtype=jnp.int32)[None, :]
    cmp_end = starts + CMP_BLOCK - 1
    k_cmp = compress_blocks(k_c.reshape(shp), idx, cmp_pe_k, cmp_w1_k, cmp_w2_k)
    v_cmp = compress_blocks(v_c.reshape(shp), idx, cmp_pe_v, cmp_w1_v, cmp_w2_v)
    k_cmp = rope(rms_norm_2(k_cmp, k_norm[0]), cmp_end)

    n_slc = S // SLC_BLOCK
    n_sel = min(SLC_TOPN, n_slc)
    s0 = np.arange(n_cmp) * CMP_STRIDE
    s1 = s0 + CMP_BLOCK
    b0 = np.arange(n_slc) * SLC_BLOCK
    b1 = b0 + SLC_BLOCK
    ov = np.clip(np.minimum(s1[:, None], b1[None, :]) - np.maximum(s0[:, None], b0[None, :]), 0, None) / CMP_BLOCK
    overlap = jnp.asarray(ov, dtype=jnp.float32)

    ks_blk = k_s.reshape(B, n_slc, SLC_BLOCK, G, dh).transpose(0, 3, 1, 2, 4)
    vs_blk = v_s.reshape(B, n_slc, SLC_BLOCK, G, dh).transpose(0, 3, 1, 2, 4)
    kw_pad = jnp.pad(k_w, ((0, 0), (WIN, 0), (0, 0), (0, 0)))
    vw_pad = jnp.pad(v_w, ((0, 0), (WIN, 0), (0, 0), (0, 0)))
    gates = jax.nn.sigmoid(gate_logits.astype(jnp.float32)).reshape(B, S, NSA_HEADS, 3)
    bi = jnp.arange(B)[:, None, None, None]
    gi = jnp.arange(G)[None, :, None, None]
    blk_ids = jnp.arange(n_slc, dtype=jnp.int32)
    QB = NSA_QBLOCK

    def body(n):
        t0 = n * QB
        t = t0 + jnp.arange(QB, dtype=jnp.int32)
        qb = lax.dynamic_slice_in_dim(q, t0, QB, axis=1).reshape(B, QB, G, HG, dh)
        sc = jnp.einsum('bqgjd,bcgd->bgjqc', qb, k_cmp).astype(jnp.float32) * scale
        valid_c = cmp_end[None, :] <= t[:, None]
        pc = jax.nn.softmax(jnp.where(valid_c, sc, NEG_INF_2), axis=-1)
        pc = jnp.where(valid_c, pc, 0.0)
        o_c = jnp.einsum('bgjqc,bcgd->bqgjd', pc.astype(dtype), v_cmp)
        imp = jnp.einsum('bgjqc,cn->bgqn', pc, overlap)
        cur = t // SLC_BLOCK
        forced = (blk_ids[None, :] == 0) | (blk_ids[None, :] == cur[:, None]) | (blk_ids[None, :] == cur[:, None] - 1)
        causal_b = blk_ids[None, :] * SLC_BLOCK <= t[:, None]
        score = jnp.where(forced, FORCE_SCORE, jnp.where(causal_b, imp, -1.0))
        _, sel = lax.top_k(score, n_sel)
        kg = ks_blk[bi, gi, sel]
        vg = vs_blk[bi, gi, sel]
        ss = jnp.einsum('bqgjd,bgqnkd->bgjqnk', qb, kg).astype(jnp.float32) * scale
        kpos = sel[..., None] * SLC_BLOCK + jnp.arange(SLC_BLOCK, dtype=jnp.int32)
        valid_s = kpos <= t[None, None, :, None, None]
        ss = jnp.where(valid_s[:, :, None], ss, NEG_INF_2).reshape(B, G, HG, QB, n_sel * SLC_BLOCK)
        ps = jax.nn.softmax(ss, axis=-1).reshape(B, G, HG, QB, n_sel, SLC_BLOCK)
        o_s = jnp.einsum('bgjqnk,bgqnkd->bqgjd', ps.astype(dtype), vg)
        kwb = lax.dynamic_slice_in_dim(kw_pad, t0, QB + WIN, axis=1)
        vwb = lax.dynamic_slice_in_dim(vw_pad, t0, QB + WIN, axis=1)
        kp = t0 - WIN + jnp.arange(QB + WIN, dtype=jnp.int32)
        dist = t[:, None] - kp[None, :]
        valid_w = (dist >= 0) & (dist < WIN) & (kp[None, :] >= 0)
        sw = jnp.einsum('bqgjd,bkgd->bgjqk', qb, kwb).astype(jnp.float32) * scale
        pw = jax.nn.softmax(jnp.where(valid_w, sw, NEG_INF_2), axis=-1)
        o_w = jnp.einsum('bgjqk,bkgd->bqgjd', pw.astype(dtype), vwb)
        gb = lax.dynamic_slice_in_dim(gates, t0, QB, axis=1).reshape(B, QB, G, HG, 3)
        o = gb[..., 0:1] * o_c + gb[..., 1:2] * o_s + gb[..., 2:3] * o_w
        return o.reshape(B, QB, NSA_HEADS * dh).astype(dtype)

    out = lax.map(body, jnp.arange(S // QB, dtype=jnp.int32))
    return out.transpose(1, 0, 2, 3).reshape(B, S, NSA_HEADS * dh)

def dilated_group(q, k, v, window, dilation):
    B, S, H, dh = q.shape
    scale = HEAD_DIM ** -0.5
    n_back = window // dilation
    L = -(-S // dilation)
    L = -(-L // DIL_BLOCK) * DIL_BLOCK
    Sp = L * dilation
    nb = L // DIL_BLOCK
    pad = ((0, 0), (0, Sp - S), (0, 0), (0, 0))

    def to_blocks(z):
        z = jnp.pad(z, pad).reshape(B, L, dilation, H, dh).transpose(0, 2, 3, 1, 4)
        return z.reshape(B, dilation, H, nb, DIL_BLOCK, dh)

    def with_prev(z):
        prev = jnp.pad(z[:, :, :, :-1], ((0, 0), (0, 0), (0, 0), (1, 0), (0, 0), (0, 0)))
        return jnp.concatenate([prev, z], axis=4)

    qb = to_blocks(q)
    kk = with_prev(to_blocks(k))
    vv = with_prev(to_blocks(v))
    s = jnp.einsum('brhnqd,brhnkd->brhnqk', qb, kk).astype(jnp.float32) * scale
    blk = jnp.arange(nb, dtype=jnp.int32)[:, None]
    pq = blk * DIL_BLOCK + jnp.arange(DIL_BLOCK, dtype=jnp.int32)[None, :]
    pk = (blk - 1) * DIL_BLOCK + jnp.arange(2 * DIL_BLOCK, dtype=jnp.int32)[None, :]
    dist = pq[:, :, None] - pk[:, None, :]
    valid = (dist >= 0) & (dist <= n_back) & (pk[:, None, :] >= 0)
    s = jnp.where(valid, s, NEG_INF_2)
    m = jnp.max(s, axis=-1, keepdims=True)
    e = jnp.exp(s - m)
    den = jnp.sum(e, axis=-1)
    o = jnp.einsum('brhnqk,brhnkd->brhnqd', e, vv.astype(jnp.float32)) / den[..., None]
    lse = m[..., 0] + jnp.log(den)
    o = o.reshape(B, dilation, H, L, dh).transpose(0, 3, 1, 2, 4).reshape(B, Sp, H, dh)[:, :S]
    lse = lse.reshape(B, dilation, H, L).transpose(0, 3, 1, 2).reshape(B, Sp, H)[:, :S]
    return o, lse

def dilated_attention(d_cols, q_norm, k_norm):
    B, S, _ = d_cols.shape
    pos = jnp.arange(S, dtype=jnp.int32)
    d = d_cols.reshape(B, S, DIL_GROUPS, 3, DIL_HEADS_PER_GROUP, HEAD_DIM)
    outs, lses = [], []
    for g, (window, dilation) in enumerate(DIL_PATTERNS):
        qg = rope(rms_norm_2(d[:, :, g, 0], q_norm[g]), pos)
        kg = rope(rms_norm_2(d[:, :, g, 1], k_norm[g]), pos)
        o, lse = dilated_group(qg, kg, d[:, :, g, 2], window, dilation)
        outs.append(o)
        lses.append(lse)
    alpha = jax.nn.softmax(jnp.stack(lses, axis=0), axis=0)
    o = jnp.sum(alpha[..., None] * jnp.stack(outs, axis=0), axis=0)
    return o.reshape(B, S, DIL_WIDTH).astype(d_cols.dtype)

def peer(hn, w_q, subkeys, u, v):
    B, S, D = hn.shape
    T = B * S
    H, K = PEER_HEADS, PEER_TOPK
    xt = hn.reshape(T, D)
    q = (xt @ w_q).reshape(T, H, 2, PEER_QDIM // 2)
    s = jnp.einsum('thcd,cnd->thcn', q, subkeys).astype(jnp.float32)
    s1, i1 = lax.top_k(s[:, :, 0], K)
    s2, i2 = lax.top_k(s[:, :, 1], K)
    cand = (s1[..., :, None] + s2[..., None, :]).reshape(T, H, K * K)
    sc, ci = lax.top_k(cand, K)
    e1 = jnp.take_along_axis(i1, ci // K, axis=-1)
    e2 = jnp.take_along_axis(i2, ci % K, axis=-1)
    idx = e1 * PEER_NKEYS + e2
    g = jax.nn.softmax(sc, axis=-1)
    C = PEER_CHUNK
    nc = T // C

    def body(args):
        xc, ic, gc = args
        a = jnp.einsum('cd,chkd->chk', xc, u[ic])
        act = (jax.nn.gelu(a.astype(jnp.float32)) * gc).astype(xc.dtype)
        return jnp.einsum('chk,chkd->cd', act, v[ic])

    out = lax.map(body, (xt.reshape(nc, C, D), idx.reshape(nc, C, H, K), g.reshape(nc, C, H, K)))
    return out.reshape(B, S, D)

def second_inputs(seed: int = 0) -> dict:
    key = jax.random.key(seed)
    ks = jax.random.split(key, 24)
    f32 = jnp.float32

    def nrm(k, shape, scale):
        return jax.random.normal(k, shape, f32) * scale

    def gain(k, shape):
        return 1.0 + 0.02 * jax.random.normal(k, shape, f32)

    flat = CMP_BLOCK * HEAD_DIM
    nsa_w = NSA_HEADS * HEAD_DIM
    return {
        "x": nrm(ks[0], (BATCH, SEQ, D_MODEL), 1.0),
        "norm1_g": gain(ks[1], (D_MODEL,)),
        "w_in": nrm(ks[2], (D_MODEL, IN_COLS), D_MODEL ** -0.5),
        "nsa_q_norm": gain(ks[3], (HEAD_DIM,)),
        "nsa_k_norm": gain(ks[4], (3, HEAD_DIM)),
        "cmp_pe_k": nrm(ks[5], (CMP_BLOCK, HEAD_DIM), 0.1),
        "cmp_w1_k": nrm(ks[6], (flat, CMP_HIDDEN), flat ** -0.5),
        "cmp_w2_k": nrm(ks[7], (CMP_HIDDEN, HEAD_DIM), CMP_HIDDEN ** -0.5),
        "cmp_pe_v": nrm(ks[8], (CMP_BLOCK, HEAD_DIM), 0.1),
        "cmp_w1_v": nrm(ks[9], (flat, CMP_HIDDEN), flat ** -0.5),
        "cmp_w2_v": nrm(ks[10], (CMP_HIDDEN, HEAD_DIM), CMP_HIDDEN ** -0.5),
        "dil_q_norm": gain(ks[11], (DIL_GROUPS, HEAD_DIM)),
        "dil_k_norm": gain(ks[12], (DIL_GROUPS, HEAD_DIM)),
        "w_up_nsa": nrm(ks[13], (nsa_w, D_MODEL), nsa_w ** -0.5),
        "w_up_dil": nrm(ks[14], (DIL_WIDTH, D_MODEL), DIL_WIDTH ** -0.5),
        "w_o": nrm(ks[15], (D_MODEL, D_MODEL), D_MODEL ** -0.5),
        "norm2_g": gain(ks[16], (D_MODEL,)),
        "peer_wq": nrm(ks[17], (D_MODEL, PEER_HEADS * PEER_QDIM), D_MODEL ** -0.5),
        "peer_subkeys": nrm(ks[18], (2, PEER_NKEYS, PEER_QDIM // 2), (PEER_QDIM // 2) ** -0.5),
        "peer_u": nrm(ks[19], (PEER_N_EXPERTS, D_MODEL), D_MODEL ** -0.5),
        "peer_v": nrm(ks[20], (PEER_N_EXPERTS, D_MODEL), PEER_HEADS ** -0.5),
    }

def second_block(x, norm1_g, w_in, nsa_q_norm, nsa_k_norm, cmp_pe_k, cmp_w1_k, cmp_w2_k,
              cmp_pe_v, cmp_w1_v, cmp_w2_v, dil_q_norm, dil_k_norm, w_up_nsa, w_up_dil,
              w_o, norm2_g, peer_wq, peer_subkeys, peer_u, peer_v):
    B, S, D = x.shape
    sizes = [NSA_Q_COLS] + [NSA_KV_COLS] * 6 + [NSA_GATE_COLS, DIL_COLS, MERGE_COLS]
    splits = [int(c) for c in np.cumsum(sizes)[:-1]]
    for _ in range(DEPTH_2):
        h = rms_norm_2(x, norm1_g)
        z = jnp.einsum('bsd,dc->bsc', h, w_in)
        q_n, kc, vc, ksl, vsl, kwn, vwn, g_nsa, dil, mg = jnp.split(z, splits, axis=-1)
        y_nsa = nsa_attention(q_n, kc, vc, ksl, vsl, kwn, vwn, g_nsa, nsa_q_norm, nsa_k_norm,
                              cmp_pe_k, cmp_w1_k, cmp_w2_k, cmp_pe_v, cmp_w1_v, cmp_w2_v)
        y_dil = dilated_attention(dil, dil_q_norm, dil_k_norm)
        gm = jax.nn.sigmoid(mg.astype(jnp.float32)).reshape(B, S, 2, D)
        merged = gm[:, :, 0] * (y_nsa @ w_up_nsa) + gm[:, :, 1] * (y_dil @ w_up_dil)
        x = x + merged.astype(x.dtype) @ w_o
        x = x + peer(rms_norm_2(x, norm2_g), peer_wq, peer_subkeys, peer_u, peer_v)
    return x


def setup_inputs(seed=0):
    out = dict(first_inputs(seed))
    for name, value in second_inputs(seed + 1).items():
        if name != "x":
            out[name + "_2"] = value
    return out


def reference(
    x, c, positions, ada_w, ada_b, norm_g, ffn_w1, ffn_w2, mla_w_in, mla_q_norm, mla_kv_norm,
    mla_w_q_up, mla_w_kv_up, mla_w_out, sb_w_in, sb_w_out, ret_w_in, ret_gn_g, ret_w_out,
    norm1_g_2, w_in_2, nsa_q_norm_2, nsa_k_norm_2, cmp_pe_k_2, cmp_w1_k_2, cmp_w2_k_2,
    cmp_pe_v_2, cmp_w1_v_2, cmp_w2_v_2, dil_q_norm_2, dil_k_norm_2, w_up_nsa_2, w_up_dil_2,
    w_o_2, norm2_g_2, peer_wq_2, peer_subkeys_2, peer_u_2, peer_v_2,
):
    x = first_block(
        x, c, positions, ada_w, ada_b, norm_g, ffn_w1, ffn_w2, mla_w_in, mla_q_norm,
        mla_kv_norm, mla_w_q_up, mla_w_kv_up, mla_w_out, sb_w_in, sb_w_out, ret_w_in, ret_gn_g,
        ret_w_out,
    )
    return second_block(
        x, norm1_g_2, w_in_2, nsa_q_norm_2, nsa_k_norm_2, cmp_pe_k_2, cmp_w1_k_2, cmp_w2_k_2,
        cmp_pe_v_2, cmp_w1_v_2, cmp_w2_v_2, dil_q_norm_2, dil_k_norm_2, w_up_nsa_2, w_up_dil_2,
        w_o_2, norm2_g_2, peer_wq_2, peer_subkeys_2, peer_u_2, peer_v_2,
    )


_drawn_inputs = setup_inputs


def setup_inputs(seed=0):
    import zlib

    import numpy as np

    out = dict(_drawn_inputs(seed))
    spreads = {}
    factors = {'mla_q_norm': 4.087,
     'ret_gn_g': 2.841,
     'norm1_g_2': 5.163,
     'nsa_q_norm_2': 8.0,
     'nsa_k_norm_2': 8.0,
     'cmp_pe_k_2': 8.0,
     'cmp_pe_v_2': 7.553,
     'dil_q_norm_2': 8.0,
     'dil_k_norm_2': 8.0,
     'norm2_g_2': 13.544}
    for name, (base, spread) in spreads.items():
        noise = np.random.default_rng([zlib.crc32(name.encode()), seed]).standard_normal(out[name].shape)
        drawn = base * np.exp(spread * noise) if base else spread * noise
        out[name] = __import__('jax').numpy.asarray(drawn.astype(out[name].dtype))
    for name, factor in factors.items():
        out[name] = (out[name] * factor).astype(out[name].dtype)
    return out
```

```python
from collections import Counter, namedtuple
from contextlib import ExitStack

import numpy as np
import concourse.bass as bass
from concourse import mybir

T = 512
D = 1024
P = 128
C = D // P
TB = T // P
FF = 4 * D
LAYERS = 4
EPS = 1e-6
NEG = -1e30
SLOT = 8 * P
RING = 4
AHEAD = 2
LIN_BANKS = 4
MLA_H, MLA_NOPE, MLA_ROPE, MLA_V = 8, 128, 64, 128
SB_H, SB_D = 16, 64
RET_H = 4
NSA_H, NSA_G, HD = 8, 2, 64
N_CMP = (T - 32) // 16 + 1
DIL_G, DIL_H = 3, 4
DILATIONS = (1, 4, 16)
PEER_H, PEER_K, NKEY = 8, 16, 128
E2_PART = 48

ADA_COLS = 1536
ADA_GROUPS = 6 * D // ADA_COLS
ARENA = 52

MIXERS = ("mla", "sb", "ret", "mla")
STAGES = tuple(s for i in range(LAYERS) for s in ((MIXERS[i], i), ("ffn", i))) + (("nsa", 4), ("peer", 4))

VEC_WIDTHS = {
    "c": C, "norm_g": LAYERS * 4 * C, "ada_b": LAYERS * 6 * C, "q_norm": 4, "kv_norm": 2,
    "gn_g": 16, "norm1": C, "norm2": C, "nsa_q": 1, "nsa_k": 3, "dil_q": 3, "dil_k": 3,
    "pe_k": 32, "pe_v": 32, "inv_mla": 1, "inv_ret": 1, "row_ok": 1,
}
VEC_AT, _n = {}, 0
for _k, _w in VEC_WIDTHS.items():
    VEC_AT[_k] = _n
    _n += _w
VEC_COLS = _n

MAT_WIDTHS = {"ident": P, "rot_mla": P, "rot_nsa": P, "pair_ones": P}
PHASE_WIDTHS = {
    "mla": {"causal": T},
    "sb": {"strict": P, "fill_future": P, "suffix": P, "minus_ones": P},
    "ret": {"decay": RET_H * T},
    "nsa": {"cos": T, "sin": T, "causal": T, "dil0": T, "dil1": T, "dil2": T, "cmp_mask": TB * 32},
    "peer": {"iota": P, "iota16": PEER_K},
}
PHASE_OFFSET = {"mla": 2 * T, "ret": 2 * T}
PHASE_COLS = 7 * T


def slots_of(stage):
    return {"mla": 4 + 1 + 1 + 3 + 8, "sb": 32, "ret": 64, "ffn": 64,
            "nsa": 4 + 4 + 12 + 16 + 8 + 1 + 16 + 1 + 4 + 2 + 8, "peer": 8 + 1 + 256}[stage[0]]


Seg = namedtuple("Seg", "products keys mask values")
Row = namedtuple("Row", "segs gate ok group qb start stop dest out_lo out_n")


def build(nc, wstream, ada, vecs, mats, phase, x_in, positions, out, stages):
    f32, f16, i32, u32 = mybir.dt.float32, mybir.dt.float16, mybir.dt.int32, mybir.dt.uint32
    ACT, ALU, AX = mybir.ActivationFunctionType, mybir.AluOpType, mybir.AxisListType
    n_slots = sum(slots_of(s) for s in stages)
    ctx = ExitStack()
    with ctx:
        def sb(name, shape, dt=f32):
            return ctx.enter_context(nc.sbuf_tensor(name, shape, dt))

        def sem(name):
            return ctx.enter_context(nc.semaphore(name))

        x = sb("x", [P, C, T])
        h = sb("h", [P, C, T])
        y = sb("y", [P, C, T])
        arena = sb("arena", [P, ARENA, T])
        ring = sb("ring", [P, RING, SLOT])
        halves = sb("halves", [P, RING, 2, SLOT], f16)
        pc = sb("pc", [P, PHASE_COLS])
        mat = sb("mat", [P, len(MAT_WIDTHS), P])
        ones = sb("ones", [P, P])
        rinv = sb("rinv", [P, T])
        tmp = sb("tmp", [P, T])
        vec = sb("vec", [P, VEC_COLS])
        cond = sb("cond", [P, C])
        mod = sb("mod", [P, 6 * C])
        gain = sb("gain", [P, 4 * C])
        small = sb("small", [P, 16])
        epsb = sb("epsb", [P, 1])
        gates = sb("gates", [P, TB, 24])
        ps = ctx.enter_context(nc.psum_tensor("ps", [P, 8, T], f32))

        ident, rot_mla, rot_nsa, pair_ones = (mat[:, i, :] for i in range(4))
        flat = arena[:, :, :].rearrange("p c t -> p (c t)")
        h16 = h[:, :, :].bitcast(f16).rearrange("p c (a t) -> p c a t", a=2)
        y16 = y[:, :, :].bitcast(f16).rearrange("p c (a t) -> p c a t", a=2)
        hidden = arena[:, 0:32, :].bitcast(f16).rearrange("p c (a t) -> p c a t", a=2)
        ada_w = flat[:, 32 * T:32 * T + 2 * ADA_COLS].rearrange("p (b n) -> p b n", b=2)
        ada_sum = flat[:, 40 * T:40 * T + 6 * D]

        def v(name, i=0, n=1):
            return vec[:, VEC_AT[name] + i:VEC_AT[name] + i + n]

        def const(kind, name):
            at = PHASE_OFFSET.get(kind, 0)
            for k, w in PHASE_WIDTHS[kind].items():
                if k == name:
                    return pc[:, at:at + w]
                at += w
            raise KeyError(name)

        s_slot = [sem(f"slot_loaded{i}") for i in range(RING)]
        s_used = sem("slot_used")
        s_tile = sem("tile_done")
        s_evac = sem("tile_read")
        s_const = sem("consts_loaded")
        s_phase = sem("phase_loaded")
        s_whigh = sem("weights_high")
        s_wlow = sem("weights_low")
        s_hhigh = sem("input_high")
        s_hlow = sem("input_low")
        s_hid = sem("hidden_high")
        s_hidl = sem("hidden_low")
        s_ones = sem("ones_set")
        s_sq = sem("squares")
        s_cond = sem("cond_ready")
        s_adaw = [sem(f"ada_loaded{i}") for i in range(2)]
        s_adas = sem("ada_step")
        s_adat = sem("ada_total")
        s_mod = sem("mod_ready")
        s_scaled = sem("scaled")
        s_h = sem("h_ready")
        s_x = sem("x_updated")
        s_vd = sem("vector_chain")
        s_ac = sem("scalar_chain")
        s_norm = sem("latent_ready")
        s_rot = sem("rotated")
        s_relu = sem("relu")
        s_tab = sem("table_arg")
        s_trig = sem("tables_ready")
        s_score = sem("scores")
        s_masked = sem("masked")
        s_nmax = sem("row_max")
        s_prob = sem("exponentials")
        s_normed = sem("probs")
        s_pt = sem("probs_transposed")
        s_ptc = sem("probs_copied")
        s_pv = sem("mixed_values")
        s_o = sem("head_out")
        s_z = sem("logits")
        s_zc = sem("logits_clamped")
        s_sp = sem("softplus")
        s_log = sem("log_one_minus")
        s_suf = sem("suffix_added")
        s_stick = sem("stick")
        s_dec = sem("decayed")
        s_gated = sem("gated")
        s_merge = sem("merged")
        s_pe = sem("pe_added")
        s_top = sem("experts_chosen")
        s_diff = sem("score_gaps")
        s_gexp = sem("gate_exps")
        s_gate_step = sem("gated_steps")
        s_same = sem("key_matches")
        s_hot = sem("one_hots")
        s_w = sem("expert_weighted")
        s_out = sem("out_stored")
        block = ctx.enter_context(nc.Block())
        totals = {}

        def mla_rows():
            rows = []
            for hd in range(MLA_H):
                half = slice(64 * (hd % 2), 64 * (hd % 2) + 64)
                for qb in range(TB):
                    q = slice(qb * P, qb * P + P)
                    n = (qb + 1) * P
                    products = [(arena[:, hd, q], arena[:, 12 + hd, 0:n]),
                                (arena[half, 8 + hd // 2, q], arena[half, 28, 0:n])]
                    values = [(P, arena[:, 20 + 2 * kb:22 + 2 * kb, :]
                               .rearrange("p a t -> p (a t)")[:, hd * P:hd * P + P]) for kb in range(qb + 1)]
                    mask = const("mla", "causal")[:, (TB - 1 - qb) * P:T]
                    rows.append(Row([Seg(products, n, mask, values)], None, None, hd, qb, True, True,
                                    arena[:, hd, :] if qb == TB - 1 else None, 0, P))
            return rows

        def nsa_rows():
            rows = []
            for j in range(4):
                for g in range(NSA_G):
                    hd = 4 * g + j
                    half = slice(64 * g, 64 * g + 64)
                    for qb in range(TB):
                        q = slice(qb * P, qb * P + P)
                        n = (qb + 1) * P
                        for br in range(3):
                            if br == 0:
                                products = [(arena[half, j, q], cmp_k[half, 0:N_CMP])]
                                mask = const("nsa", "cmp_mask")[:, 32 * qb:32 * qb + N_CMP]
                                seg = Seg(products, N_CMP, mask, [(N_CMP, cmp_v[0:N_CMP, 64 * g:64 * g + 64])])
                            else:
                                products = [(arena[half, j, q], arena[half, 3 + br, 0:n])]
                                at = 128 * (br - 1) + 64 * g
                                seg = Seg(products, n, const("nsa", "causal")[:, (TB - 1 - qb) * P:T],
                                          [(P, nat(kb)[:, at:at + 64]) for kb in range(qb + 1)])
                            ok = v("row_ok") if br == 0 and qb == 0 else None
                            rows.append(Row([seg], gates[:, qb, 3 * hd + br:3 * hd + br + 1], ok,
                                            hd, qb, br == 0, br == 2,
                                            arena[half, j, :] if qb == TB - 1 and br == 2 else None, 64 * g, 64))
            for hd in range(DIL_H):
                half = slice(64 * (hd % 2), 64 * (hd % 2) + 64)
                for qb in range(TB):
                    q = slice(qb * P, qb * P + P)
                    n = (qb + 1) * P
                    segs = []
                    for g in range(DIL_G):
                        at = 256 + 256 * g + 64 * hd
                        segs.append(Seg([(arena[half, 8 + 4 * g + hd // 2, q],
                                          arena[half, 10 + 4 * g + hd // 2, 0:n])], n,
                                        const("nsa", f"dil{g}")[:, (TB - 1 - qb) * P:T],
                                        [(P, nat(kb)[:, at:at + 64]) for kb in range(qb + 1)]))
                    rows.append(Row(segs, None, None, 8 + hd, qb, True, True,
                                    arena[half, 8 + hd // 2, :] if qb == TB - 1 else None, 64 * (hd % 2), 64))
            return rows

        cmp_k = arena[:, 48, 0:32]
        cmp_v = arena[:, 48, 64:192]
        cmp_h = arena[:, 48, 192:192 + 8 * 32].rearrange("p (a c) -> p a c", a=8)

        def nat(kb):
            return arena[:, 20 + 2 * kb:22 + 2 * kb, :].rearrange("p a t -> p (a t)")

        def next_layer(at):
            return any(s[1] == at + 1 and s[1] < LAYERS for s in stages)

        def nsa_units():
            cos, sin = const("nsa", "cos"), const("nsa", "sin")
            units = [(arena[:, j, :], v("nsa_q"), T, cos, sin, True) for j in range(4)]
            units += [(arena[:, 3 + i, :], v("nsa_k", i), T, cos, sin, False) for i in (1, 2)]
            for g in range(DIL_G):
                units += [(arena[:, 8 + 4 * g + i, :], v("dil_q", g), T, cos, sin, True) for i in range(2)]
                units += [(arena[:, 10 + 4 * g + i, :], v("dil_k", g), T, cos, sin, False) for i in range(2)]
            units.append((cmp_k[:, 0:N_CMP], v("nsa_k", 0), N_CMP, cos[:, 31:T:16], sin[:, 31:T:16], False))
            return units

        key_scores = flat[:, 8 * T:24 * T].rearrange("p (b h c n) -> p b h c n", b=TB, h=PEER_H, c=2)
        cand = flat[:, 24 * T:28 * T].rearrange("p (h n) -> p h n", h=PEER_H)
        match = flat[:, 28 * T:32 * T].rearrange("p (h k a) -> p h k a", h=PEER_H, k=PEER_K)
        pick = flat[:, 32 * T:36 * T].rearrange("p (a n) -> p a n", n=P)
        top_v = flat[:, 32 * T:32 * T + 256].rearrange("p (h c k) -> p h c k", h=PEER_H, c=2)
        top_i = flat[:, 32 * T + 256:33 * T].bitcast(u32).rearrange("p (h c k) -> p h c k", h=PEER_H, c=2)
        top_f = flat[:, 33 * T:33 * T + 256].rearrange("p (h c k) -> p h c k", h=PEER_H, c=2)
        best_v, best_i = pick[:, 6, :], pick[:, 7, :].bitcast(u32)
        digit_i, digit_f = pick[:, 8, :].bitcast(u32), pick[:, 9, :]
        expert = [pick[:, 10, :], pick[:, 11, :], pick[:, 12, :]]
        exps = pick[:, 13, :]
        chosen = arena[:, 48:50, :].bitcast(f16).rearrange("p c (a t) -> p (c a) t", a=2)
        gate32, gated = arena[:, 50, :], arena[:, 51, :]
        part_gates = arena[:, 0:E2_PART, :]
        HOT = 8
        hots = pc[:, T:7 * T].bitcast(f16)
        hot1 = hots[:, 0:2 * HOT * P].rearrange("p (b j n) -> p b j n", b=2, j=HOT)
        hot2 = hots[:, 2 * HOT * P:2 * HOT * (P + 2 * E2_PART)].rearrange("p (b a n) -> p b a n", b=2, a=2)
        same2 = hots[:, 2 * HOT * (P + 2 * E2_PART):2 * HOT * (P + 2 * E2_PART) + HOT * E2_PART]
        iota_h = hots[:, 2 * HOT * (P + 2 * E2_PART) + HOT * E2_PART:2 * HOT * (P + 2 * E2_PART) + HOT * E2_PART + P]
        PARTS = [(lo, min(E2_PART, NKEY - lo)) for lo in range(0, NKEY, E2_PART)]

        def row_buf(region, i):
            return region[:, 3 * (i % 2):3 * (i % 2) + 3, :]

        @block.sync
        def _(sp):
            for j in range(min(RING, n_slots)):
                sp.dma_start(ring[:, j, :], wstream[j]).then_inc(s_slot[j], 16)
            whole = n_slots // RING
            if whole > 1:
                with sp.Fori(1, whole) as i:
                    for j in range(RING):
                        sp.wait_ge(s_used, (i - 1) * RING + j + 1)
                        sp.dma_start(ring[:, j, :], wstream[i * RING + j]).then_inc(s_slot[j], 16)
            for n in range(max(whole, 1) * RING, n_slots):
                sp.wait_ge(s_used, n - RING + 1)
                sp.dma_start(ring[:, n % RING, :], wstream[n]).then_inc(s_slot[n % RING], 16)
            sp.wait_ge(s_x, C * x_updates(stages))
            sp.dma_start(out, x[:, :, :]).then_inc(s_out, 16)
            sp.wait_ge(s_out, 16)

        @block.gpsimd
        def _(pool):
            def ada_load(nth):
                base = nth * ADA_GROUPS * C
                if nth == 0:
                    for n in range(C):
                        if n >= 2:
                            pool.wait_ge(s_adas, n - 1)
                        pool.dma_start(ada_w[:, n % 2, :], ada[n]).then_inc(s_adaw[n % 2], 16)
                with pool.Fori(1 if nth == 0 else 0, ADA_GROUPS) as g:
                    for n in range(C):
                        pool.wait_ge(s_adas, g * C + (base + n - 1))
                        pool.dma_start(ada_w[:, n % 2, :], ada[g * C + (base + n)]).then_inc(s_adaw[n % 2], 16)

            pool.dma_start(vec[:, :], vecs).then_inc(s_const, 16)
            pool.dma_start(x[:, :, :], x_in).then_inc(s_const, 16)
            pool.dma_start(mat[:, :, :], mats).then_inc(s_const, 16)
            nc.gpsimd.memset(ones[:, :], 1.0).then_inc(s_ones, 1)
            nc.gpsimd.memset(epsb[:, :], EPS).then_inc(s_ones, 1)
            if stages[0][1] < LAYERS:
                ada_load(0)
            last_layer = max([s[1] for s in stages if s[1] < LAYERS], default=-1)
            first_layer = stages[0][1]
            for n, (kind, at) in enumerate(stages):
                if kind in PHASE_WIDTHS:
                    if n:
                        pool.wait_ge(s_x, C * n)
                    lo = PHASE_OFFSET.get(kind, 0)
                    wide = sum(PHASE_WIDTHS[kind].values())
                    pool.dma_start(pc[:, lo:lo + wide], phase[kind]).then_inc(s_phase, 16)
                    if kind in PHASE_OFFSET:
                        pool.dma_start(pc[:, 6 * T:7 * T].bitcast(i32), positions.to_broadcast([P, T]))\
                            .then_inc(s_phase, 16)
                elif kind == "ffn" and at < last_layer:
                    ada_load(at + 1 - first_layer)

        @block.tensor
        def _(pe):
            seen = Counter()

            def bank():
                t = seen["tile"]
                if t >= LIN_BANKS:
                    pe.wait_ge(s_evac, t - LIN_BANKS + 1)
                seen["tile"] += 1
                return ps[:, t % LIN_BANKS, :]

            def slot():
                n = seen["slot"]
                pe.wait_ge(s_slot[n % RING], 16 * (n // RING + 1))
                seen["slot"] += 1
                return ring[:, n % RING, :]

            def wait(s, key, n=0):
                seen[key] += n
                if seen[key]:
                    pe.wait_ge(s, seen[key])

            def sum_squares(squares, stat=None, n=T):
                b = bank()
                for k, sq in enumerate(squares):
                    wait(s_sq, "sq", 1)
                    mm = nc.tensor.matmul(b[:, 0:n], ones[:, :] if stat is None else stat, sq,
                                          start=(k == 0), stop=(k == len(squares) - 1))
                mm.then_inc(s_tile, 1)

            def linear(inputs, tiles, ready=None, waits=()):
                for m in range(tiles):
                    b = bank()
                    for k, a in enumerate(inputs):
                        if k % 8 == 0:
                            w = slot()
                        if m == 0 and ready is not None:
                            wait(ready[0], ready[1], 1)
                        mm = nc.tensor.matmul(b, w[:, (k % 8) * P:(k % 8 + 1) * P], a,
                                              start=(k == 0), stop=(k == len(inputs) - 1))
                        if k % 8 == 7:
                            mm.then_inc(s_used, 1)

            def linear_tokens(halves):
                for _ in range(halves):
                    banks = [bank() for _ in range(TB)]
                    for s in range(4):
                        w = slot()
                        for tb in range(TB):
                            for k in range(2):
                                mm = nc.tensor.matmul(banks[tb], h[:, 2 * s + k, tb * P:tb * P + P],
                                                      w[:, k * T:k * T + T],
                                                      start=(s + k == 0), stop=(s == 3 and k == 1))
                        mm.then_inc(s_used, 1)

            def rotate(src, stat, n=T):
                b = bank()
                wait(s_norm, "norm", 1)
                nc.tensor.matmul(b[:, 0:n], stat, src[:, 0:n], start=True, stop=True).then_inc(s_tile, 1)

            def norm_rope(units):
                for i in range(len(units) + 1):
                    if i < len(units):
                        sum_squares([tmp[:, 0:units[i][2]]], pair_ones, units[i][2])
                    if i:
                        rotate(units[i - 1][0], rot_nsa, units[i - 1][2])

            def row_blocks(rows):
                pe.wait_ge(s_evac, seen["tile"])
                base_seg, base_pt, base_group, base_row = seen["seg"], seen["pt"], seen["group"], seen["row"]
                group_of = list(dict.fromkeys(r.group for r in rows))
                for i in range(len(rows) + 3):
                    if i < len(rows):
                        for sg in rows[i].segs:
                            g = seen["seg"]
                            if g - base_seg >= 3:
                                pe.wait_ge(s_masked, seen["mask"] + g - base_seg - 2)
                            for k, (a, b) in enumerate(sg.products):
                                mm = nc.tensor.matmul(ps[:, g % 3, 0:sg.keys], a, b, start=(k == 0),
                                                      stop=(k == len(sg.products) - 1))
                            mm.then_inc(s_score, 1)
                            seen["seg"] += 1
                    if 2 <= i < len(rows) + 2:
                        r = rows[i - 2]
                        pe.wait_ge(s_normed, base_row + i - 1)
                        at = 0
                        for sg in r.segs:
                            g = seen["pt"]
                            if g - base_pt >= 3:
                                pe.wait_ge(s_ptc, g - 2)
                            src = row_buf(h, i - 2).rearrange("p a t -> p (a t)")
                            for kb, (nk, _) in enumerate(sg.values):
                                mm = nc.tensor.transpose(ps[0:nk, 3 + g % 3, kb * P:kb * P + P],
                                                         src[:, at:at + nk], ident)
                                at += nk
                            mm.then_inc(s_pt, 1)
                            seen["pt"] += 1
                    if i >= 3:
                        r = rows[i - 3]
                        gi = group_of.index(r.group)
                        if r.qb == 0 and r.start and gi >= 2:
                            pe.wait_ge(s_o, base_group + gi - 1)
                        seen["ptc"] += len(r.segs)
                        pe.wait_ge(s_ptc, seen["ptc"])
                        o = ps[r.out_lo:r.out_lo + r.out_n, 6 + gi % 2, r.qb * P:r.qb * P + P]
                        pt = row_buf(y, i - 3)
                        todo = [(s, kb, nk, va) for s, sg in enumerate(r.segs) for kb, (nk, va) in enumerate(sg.values)]
                        for k, (s, kb, nk, va) in enumerate(todo):
                            mm = nc.tensor.matmul(o, va, pt[0:nk, s, kb * P:kb * P + P],
                                                  start=(r.start and k == 0), stop=(r.stop and k == len(todo) - 1))
                        mm.then_inc(s_pv, 1)
                seen["row"] += len(rows)
                seen["mask"] += seen["seg"] - base_seg
                seen["group"] += len(group_of)
                pe.wait_ge(s_o, seen["group"])

            def ada_sums():
                seen["ada"] += ADA_GROUPS * C
                pe.wait_ge(s_adas, seen["ada"])
                b = bank()
                for j in range(6 * C):
                    mm = nc.tensor.matmul(b[:, j:j + 1], ada_sum[:, j * P:j * P + P], ones[:, 0:1],
                                          start=True, stop=True)
                mm.then_inc(s_tile, 1)

            def mla(layer):
                sum_squares([h[:, k, :] for k in range(C)])
                linear([h[:, k, :] for k in range(C)], 4, (s_h, "h"))
                sum_squares([y[:, 4 + k, :] for k in range(2)])
                sum_squares([y[:, 6, :]])
                b = bank()
                pe.wait_ge(s_evac, seen["tile"] - 3)
                nc.tensor.matmul(b, rot_mla, arena[:, 28, :], start=True, stop=True).then_inc(s_tile, 1)
                wait(s_norm, "norm", 3)
                w = slot()
                for m in range(8):
                    b = bank()
                    mm = nc.tensor.matmul(b, w[:, m * P:m * P + P], arena[:, 31, :], start=True, stop=True)
                    mm.then_inc(s_used if m == 7 else s_tile, 1)
                w = slot()
                for tb in range(TB):
                    for half in range(2):
                        b = bank()
                        mm = nc.tensor.matmul(b, arena[:, 31, tb * P:tb * P + P], w[:, half * T:half * T + T],
                                              start=True, stop=True)
                        mm.then_inc(s_used if tb == TB - 1 and half else s_tile, 1)
                for m in range(12):
                    b = bank()
                    if m % 4 == 0:
                        w = slot()
                    for k in range(2):
                        at = (m % 4) * 2 + k
                        mm = nc.tensor.matmul(b, w[:, at * P:at * P + P], arena[:, 29 + k, :],
                                              start=(k == 0), stop=(k == 1))
                    mm.then_inc(s_used if m % 4 == 3 else s_tile, 1)
                for m in range(4):
                    b = bank()
                    pe.wait_ge(s_evac, seen["tile"] - 4)
                    nc.tensor.matmul(b, rot_mla, arena[:, 8 + m, :], start=True, stop=True).then_inc(s_tile, 1)
                wait(s_rot, "rot", 5)
                row_blocks(mla_rows())
                linear([arena[:, k, :] for k in range(C)], 8)
                sum_squares([h[:, k, :] for k in range(C)])

            def split_tile(out_, buf, slot_cols, act16, first, last):
                high, low = halves[:, buf, 0, slot_cols], halves[:, buf, 1, slot_cols]
                nc.tensor.matmul(out_, high, act16[:, 0, :], start=first, stop=False)
                nc.tensor.matmul(out_, high, act16[:, 1, :], start=False, stop=False)
                return nc.tensor.matmul(out_, low, act16[:, 0, :], start=False, stop=last)

            def ffn(layer, with_ada):
                sum_squares([h[:, k, :] for k in range(C)])
                wait(s_hlow, "hlow", C)
                t0, n0 = seen["tile"], seen["split"]
                with pe.Fori(0, FF // P // 8) as i:
                    for j in range(8):
                        pe.wait_ge(s_evac, i * 8 + (t0 + j - LIN_BANKS + 1))
                        pe.wait_ge(s_wlow, i * 8 + (n0 + j + 1))
                        for k in range(C):
                            mm = split_tile(ps[:, (t0 + j) % LIN_BANKS, :], (seen["slot"] + j) % RING,
                                            slice(k * P, k * P + P), h16[:, k], k == 0, k == C - 1)
                        mm.then_inc(s_used, 1)
                seen["tile"] += FF // P
                seen["slot"] += FF // P
                seen["split"] += FF // P
                wait(s_hidl, "hid", FF // P)
                t0, n0 = seen["tile"], seen["split"]
                with pe.Fori(0, 2) as i:
                    for m in range(4):
                        pe.wait_ge(s_evac, i * 4 + (t0 + m - LIN_BANKS + 1))
                        for s in range(4):
                            j = 4 * m + s
                            pe.wait_ge(s_wlow, i * 16 + (n0 + j + 1))
                            for k in range(8):
                                mm = split_tile(ps[:, (t0 + m) % LIN_BANKS, :], (seen["slot"] + j) % RING,
                                                slice(k * P, k * P + P), hidden[:, 8 * s + k],
                                                s + k == 0, s == 3 and k == 7)
                            mm.then_inc(s_used, 1)
                seen["tile"] += C
                seen["slot"] += FF // P
                seen["split"] += FF // P
                if with_ada:
                    ada_sums()
                sum_squares([h[:, k, :] for k in range(C)])

            def stick_breaking():
                sum_squares([h[:, k, :] for k in range(C)])
                linear([h[:, k, :] for k in range(C)], 16, (s_h, "h"))
                linear_tokens(2)
                pe.wait_ge(s_evac, seen["tile"])
                wait(s_phase, "phase")
                jobs = [(hd, kb) for hd in range(SB_H) for kb in (3, 2, 1, 0)]

                def logits(n):
                    hd, kb = jobs[n]
                    half = slice(64 * (hd % 2), 64 * (hd % 2) + 64)
                    if n >= 6:
                        pe.wait_ge(s_stick, n - 5)
                    nc.tensor.matmul(ps[:, n % 6, 0:T - kb * P], arena[half, 8 + hd // 2, kb * P:kb * P + P],
                                     arena[half, hd // 2, kb * P:T], start=True, stop=True,
                                     skip_group_check=True).then_inc(s_z, 1)

                def suffix(n):
                    hd, kb = jobs[n]
                    w = T - kb * P
                    pe.wait_ge(s_log, n + 1)
                    b = ps[:, n % 6, :]
                    nc.tensor.matmul(b[:, 0:w], const("sb", "suffix"), h[:, 4 * (hd % 2) + kb, 0:w], start=False, stop=False,
                                     skip_group_check=True)
                    for later in range(kb + 1, TB):
                        nc.tensor.matmul(b[:, (later - kb) * P:w], const("sb", "minus_ones"),
                                         h[:, 4 * (hd % 2) + later, 0:T - later * P],
                                         start=False, stop=False, skip_group_check=True)
                    nc.tensor.matmul(b[:, 0:P], ident, const("sb", "fill_future"), start=False, stop=True,
                                     skip_group_check=True).then_inc(s_suf, 1)

                def mixed(hd):
                    pe.wait_ge(s_stick, 4 * hd + 4)
                    if hd >= 2:
                        pe.wait_ge(s_o, hd - 1 + seen["group"])
                    lo = 64 * (hd % 2)
                    for kb in range(TB):
                        mm = nc.tensor.matmul(ps[lo:lo + 64, 6 + hd % 2, kb * P:T],
                                              nat(kb)[:, hd * 64:hd * 64 + 64],
                                              y[:, 4 * (hd % 2) + kb, 0:T - kb * P],
                                              start=(kb == 0), stop=(kb == TB - 1), skip_group_check=True)
                    mm.then_inc(s_pv, 1)

                for n in range(len(jobs) + 4):
                    if n < len(jobs):
                        logits(n)
                    if 2 <= n < len(jobs) + 2:
                        suffix(n - 2)
                    if n >= 7 and (n - 7) % 4 == 0 and (n - 7) // 4 < SB_H:
                        mixed((n - 7) // 4)
                seen["group"] += SB_H
                pe.wait_ge(s_o, seen["group"])
                linear([arena[:, k, :] for k in range(C)], 8)
                sum_squares([h[:, k, :] for k in range(C)])

            def retention():
                sum_squares([h[:, k, :] for k in range(C)])
                for hd in range(RET_H):
                    linear([h[:, k, :] for k in range(C)], 4, (s_h, "h") if hd == 0 else None)
                    linear_tokens(1)
                    linear([h[:, k, :] for k in range(C)], 4)
                    wait(s_rot, "rot", 4)
                    for kb in range(TB):
                        n = seen["dec"]
                        if n >= 2:
                            pe.wait_ge(s_dec, n - 1)
                        for k in range(2):
                            mm = nc.tensor.matmul(ps[:, 4 + n % 2, 0:T - kb * P],
                                                  arena[:, 18 + k, kb * P:kb * P + P], arena[:, 16 + k, kb * P:T],
                                                  start=(k == 0), stop=(k == 1))
                        mm.then_inc(s_score, 1)
                        seen["seg"] += 1
                        seen["dec"] += 1
                    pe.wait_ge(s_dec, seen["dec"])
                    pe.wait_ge(s_evac, seen["tile"])
                    for m in range(4):
                        n = seen["rv"]
                        if n >= 2:
                            pe.wait_ge(s_o, seen["group"] - 1)
                        for kb in range(TB):
                            mm = nc.tensor.matmul(ps[:, 6 + n % 2, kb * P:T],
                                                  arena[:, 20 + kb, m * P:m * P + P],
                                                  arena[:, 28 + kb, 0:T - kb * P],
                                                  start=(kb == 0), stop=(kb == TB - 1), skip_group_check=True)
                        mm.then_inc(s_pv, 1)
                        seen["rv"] += 1
                        seen["group"] += 1
                    sum_squares([y[:, 4 + k, :] for k in range(4)])
                wait(s_gated, "gated", RET_H * 4)
                linear([arena[:, k, :] for k in range(16)], 8)
                sum_squares([h[:, k, :] for k in range(C)])

            def nsa():
                sum_squares([h[:, k, :] for k in range(C)])
                linear([h[:, k, :] for k in range(C)], 4 + 4 + 12 + 16, (s_h, "h"))
                linear_tokens(2)
                b = bank()
                w = slot()
                for tb in range(TB):
                    for k in range(C):
                        mm = nc.tensor.matmul(b[:, tb * P:tb * P + P], h[:, k, tb * P:tb * P + P],
                                              w[:, k * P:k * P + P], start=(k == 0), stop=(k == C - 1))
                mm.then_inc(s_used, 1)
                wait(s_pe, "pe", 4)
                for kind in range(2):
                    for m in range(2):
                        banks = [bank(), bank()]
                        for t in range(32):
                            if t % 8 == 0:
                                w = slot()
                            src = arena[:, 44 + 2 * kind + t // 16, :].rearrange("p (c s) -> p c s", s=16)
                            for g in range(NSA_G):
                                half = slice(64 * g, 64 * g + 64)
                                mm = nc.tensor.matmul(banks[g][:, 0:N_CMP], w[half, (t % 8) * P:(t % 8 + 1) * P],
                                                      src[half, t // 16:t // 16 + N_CMP, t % 16],
                                                      start=(t == 0), stop=(t == 31))
                            if t % 8 == 7:
                                mm.then_inc(s_used, 1)
                w = slot()
                b = bank()
                pe.wait_ge(s_evac, seen["tile"] - 1)
                for g in range(NSA_G):
                    for m in range(2):
                        mm = nc.tensor.matmul(b[64 * g:64 * g + 64, 0:N_CMP], w[:, 64 * m:64 * m + 64],
                                              cmp_h[:, 2 * m + g, 0:N_CMP], start=(m == 0), stop=(m == 1))
                mm.then_inc(s_tile, 1)
                b = bank()
                for g in range(NSA_G):
                    for m in range(2):
                        mm = nc.tensor.matmul(b[0:N_CMP, 64 * g:64 * g + 64], cmp_h[:, 4 + 2 * m + g, 0:N_CMP],
                                              w[:, 128 + 64 * m:192 + 64 * m], start=(m == 0), stop=(m == 1))
                mm.then_inc(s_used, 1)
                norm_rope(nsa_units())
                wait(s_rot, "rot", len(nsa_units()))
                row_blocks(nsa_rows())
                w = None
                for m in range(8):
                    b = bank()
                    if m % 2 == 0:
                        w = slot()
                    for k in range(4):
                        at = (m % 2) * 4 + k
                        mm = nc.tensor.matmul(b, w[:, at * P:at * P + P], arena[:, k, :],
                                              start=(k == 0), stop=(k == 3))
                    mm.then_inc(s_used if m % 2 else s_tile, 1)
                for m in range(8):
                    b = bank()
                    if m % 4 == 0:
                        w = slot()
                    for k in range(2):
                        at = (m % 4) * 2 + k
                        mm = nc.tensor.matmul(b, w[:, at * P:at * P + P], arena[:, 8 + k, :],
                                              start=(k == 0), stop=(k == 1))
                    mm.then_inc(s_used if m % 4 == 3 else s_tile, 1)
                wait(s_merge, "merge", C)
                linear([h[:, k, :] for k in range(C)], 8)

            def experts():
                sum_squares([h[:, k, :] for k in range(C)])
                linear([y[:, k, :] for k in range(C)], 8, (s_h, "h"))
                wait(s_hlow, "hlow", C)
                pe.wait_ge(s_evac, seen["tile"])
                w = slot()
                for tb in range(TB):
                    for four in range(4):
                        b = bank()
                        half = slice(64 * (four % 2), 64 * (four % 2) + 64)
                        for i in range(4):
                            hd = 4 * (four // 2) + i
                            mm = nc.tensor.matmul(b[:, i * P:i * P + P], arena[half, hd, tb * P:tb * P + P],
                                                  w[half, 0:P], start=True, stop=True)
                        mm.then_inc(s_used if tb == TB - 1 and four == 3 else s_tile, 1)
                for tb in range(TB):
                    b = bank()
                    wait(s_top, "top", 1)
                    for i in range(3):
                        mm = nc.tensor.transpose(b[:, i * P:i * P + P], expert[i], ident)
                    mm.then_inc(s_tile, 1)
                for lo, n in PARTS:
                    t0, b0 = seen["tile"], seen["hot"]
                    with pe.Fori(0, T // HOT // 4) as i:
                        for j in range(4):
                            pe.wait_ge(s_evac, i * 4 + (t0 + j - LIN_BANKS + 1))
                            pe.wait_ge(s_hot, i * 4 + (b0 + j + 1))
                            for t in range(HOT):
                                for part in range(2):
                                    mm = nc.tensor.matmul(ps[:, (t0 + j) % LIN_BANKS, t * n:t * n + n],
                                                          hot1[:, j % 2, t, :], hot2[:, j % 2, part, t * n:t * n + n],
                                                          start=(part == 0), stop=(part == 1))
                            mm.then_inc(s_tile, 1)
                    seen["tile"] += T // HOT
                    seen["hot"] += T // HOT
                    t0, n0, w0, x0 = seen["tile"], seen["split"], seen["w"], seen["xp"]
                    with pe.Fori(0, n // 8) as i:
                        for j in range(8):
                            pe.wait_ge(s_evac, i * 8 + (t0 + j - LIN_BANKS + 1))
                            pe.wait_ge(s_wlow, i * 16 + (n0 + j + 1))
                            for k in range(C):
                                mm = split_tile(ps[:, (t0 + j) % LIN_BANKS, :], (seen["slot"] + j) % RING,
                                                slice(k * P, k * P + P), h16[:, k], k == 0, k == C - 1)
                            mm.then_inc(s_used, 1)
                        for m in range(C):
                            pe.wait_ge(s_x, i * 8 + (seen["x"] + x0 + m - 3))
                            pe.wait_ge(s_wlow, i * 16 + (n0 + 8 + m + 1))
                            for j in range(8):
                                if m == 0:
                                    pe.wait_ge(s_w, i * 8 + (w0 + j + 1))
                                mm = split_tile(ps[:, 4 + m % 4, :], (seen["slot"] + m) % RING,
                                                slice(j * P, j * P + P), y16[:, j], j == 0, j == 7)
                            mm.then_inc(s_used, 1)
                    seen["split"] += 2 * n
                    seen["tile"] += n
                    seen["slot"] += 2 * n
                    seen["w"] += n
                    seen["xp"] += n

            nc_tab = {"mla": lambda l: mla(l), "sb": lambda l: stick_breaking(), "ret": lambda l: retention(),
                      "nsa": lambda l: nsa()}
            pe.wait_ge(s_const, 48)
            pe.wait_ge(s_ones, 2)
            if stages[0][1] < LAYERS:
                ada_sums()
            for n, (kind, at) in enumerate(stages):
                if kind in PHASE_WIDTHS:
                    seen["phase"] += 32 if kind in PHASE_OFFSET else 16
                if kind == "ffn":
                    ffn(at, next_layer(at))
                elif kind == "peer":
                    experts()
                else:
                    nc_tab[kind](at)
                seen["x"] += C
            totals["pe"] = seen

        @block.scalar
        def _(act):
            seen = Counter()

            def wait_count(s, value):
                act.wait_ge(s, value)
                act.wait_ge(s_ones, 2)

            def tile(slots=0):
                if slots:
                    seen["used"] += slots
                    act.wait_ge(s_used, seen["used"])
                else:
                    seen["tl"] += 1
                    act.wait_ge(s_tile, seen["tl"])
                t = seen["tile"]
                seen["tile"] += 1
                return ps[:, t % LIN_BANKS, :]

            def copy(dst, slots=0, scale=1.0, func=ACT.Copy, n=T):
                b = tile(slots)
                nc.scalar.activation(dst, b[:, 0:n], func, scale=scale).then_inc(s_evac, 1)

            def square(dst, src):
                nc.scalar.activation(dst, src, ACT.Square).then_inc(s_sq, 1)
                seen["sq"] += 1

            def rms(dst, features, n=T):
                b = tile()
                nc.scalar.activation(dst[:, 0:n], b[:, 0:n], ACT.Sqrt, scale=1.0 / features,
                                     bias=epsb[:, 0:1]).then_inc(s_evac, 1)

            def input_norm(shift):
                for k in range(C):
                    if seen["x"]:
                        act.wait_ge(s_x, seen["x"] - C + k + 1)
                    square(h[:, k, :], x[:, k, :])
                rms(rinv, D)
                if shift is not None:
                    for k in range(C):
                        act.wait_ge(s_scaled, seen["scaled"] + k + 1)
                        nc.scalar.activation(h[:, k, :], h[:, k, :], ACT.Identity,
                                             bias=mod[:, shift + k:shift + k + 1]).then_inc(s_h, 1)
                    seen["scaled"] += C
                seen["h"] += C

            def weights_high(n, loops=0, slots=0):
                at = seen["used"] + n
                act.wait_ge(s_slot[at % RING], loops * (16 * slots // RING) + 16 * (at // RING + 1))
                nc.scalar.activation(halves[:, at % RING, 0, :], ring[:, at % RING, :], ACT.Copy,
                                     scale=W_SCALE).then_inc(s_whigh, 1)

            def split_input(shift):
                for k in range(C):
                    if seen["x"]:
                        act.wait_ge(s_x, seen["x"] - C + k + 1)
                    square(h[:, k, :], x[:, k, :])
                for n in range(AHEAD):
                    weights_high(n)
                rms(rinv, D)
                for k in range(C):
                    act.wait_ge(s_scaled, seen["scaled"] + k + 1)
                    nc.scalar.activation(y[:, k, :], y[:, k, :], ACT.Identity,
                                         bias=mod[:, shift + k:shift + k + 1]).then_inc(s_ac, 1)
                    seen["ac"] += 1
                    act.wait_ge(s_ac, seen["ac"])
                    nc.scalar.activation(h16[:, k, 0], y[:, k, :], ACT.Copy).then_inc(s_hhigh, 1)
                seen["scaled"] += C

            def output(slots=1):
                for k in range(C):
                    b = tile(slots)
                    square(h[:, k, :], b)
                    nc.scalar.activation(y[:, k, :], b, ACT.Copy).then_inc(s_evac, 1)
                rms(rinv, D)

            def trig():
                for i in range(2):
                    seen["tab"] += 1
                    act.wait_ge(s_tab, seen["tab"])
                    nc.scalar.activation(pc[:, i * T:i * T + T], pc[:, i * T:i * T + T], ACT.Sin).then_inc(s_trig, 1)

            def row_blocks(rows):
                base_row, base_pv = seen["row"], seen["pv"]
                gi = 0
                for i in range(len(rows) + 4):
                    if i < len(rows):
                        r = rows[i]
                        keys = sum(sg.keys for sg in r.segs)
                        buf = row_buf(h, i).rearrange("p a t -> p (a t)")[:, 0:keys]
                        act.wait_ge(s_nmax, base_row + i + 1)
                        nc.scalar.activation(buf, buf, ACT.Exp, bias=small[:, i % 4:i % 4 + 1],
                                             accum_out=small[:, 4 + i % 4:5 + i % 4]).then_inc(s_prob, 1)
                    if 2 <= i < len(rows) + 2:
                        r = rows[i - 2]
                        if i >= 4:
                            act.wait_ge(s_pv, base_pv + i - 3)
                        for s, sg in enumerate(r.segs):
                            g = seen["pt"]
                            act.wait_ge(s_pt, g + 1)
                            nk = sg.values[0][0]
                            n = P * len(sg.values)
                            nc.scalar.activation(row_buf(y, i - 2)[0:nk, s, 0:n], ps[0:nk, 3 + g % 3, 0:n],
                                                 ACT.Copy).then_inc(s_ptc, 1)
                            seen["pt"] += 1
                    if i >= 4 and rows[i - 4].dest is not None:
                        r = rows[i - 4]
                        act.wait_ge(s_pv, base_pv + i - 3)
                        nc.scalar.activation(r.dest, ps[r.out_lo:r.out_lo + r.out_n, 6 + gi % 2, :],
                                             ACT.Copy).then_inc(s_o, 1)
                        gi += 1
                seen["row"] += len(rows)
                seen["pv"] += len(rows)

            def mla():
                input_norm(0)
                trig()
                copy(arena[:, 29, :], 1)
                copy(arena[:, 30, :], 1)
                copy(arena[:, 31, :], 1)
                for k in range(3):
                    act.wait_ge(s_evac, seen["tile"] - 2 + k)
                    square(y[:, 4 + k, :], arena[:, 29 + k, :])
                copy(arena[:, 28, :], 1)
                rms(rinv, 256)
                rms(tmp, 128)
                copy(y[:, 3, :])
                for m in range(8):
                    copy(arena[:, 12 + m, :], int(m == 7))
                for m in range(8):
                    copy(arena[:, 20 + m, :], int(m == 7))
                scale = (MLA_NOPE + MLA_ROPE) ** -0.5
                for m in range(12):
                    copy(arena[:, m, :], int(m % 4 == 3), scale=scale)
                for m in range(4):
                    copy(y[:, 4 + m, :])
                seen["norm"] += 3
                seen["rot"] += 5
                row_blocks(mla_rows())
                output()

            def ffn(with_ada):
                split_input(3 * C)
                t0, u0, r0, d0 = seen["tile"], seen["used"], seen["relu"], seen["hid"]
                with act.Fori(0, FF // P // 8) as i:
                    for j in range(8):
                        weights_high(j + AHEAD, i, 8)
                        relu = (rinv, tmp)[j % 2][:, :]
                        if d0 or j >= 2:
                            act.wait_ge(s_hidl, i * 8 + (d0 + j - 1))
                        else:
                            act.wait_ge(s_hidl, i * 8)
                        wait_count(s_used, i * 8 + (u0 + j + 1))
                        nc.scalar.activation(relu, ps[:, (t0 + j) % LIN_BANKS, :], ACT.Relu,
                                             scale=1.0 / W_SCALE).then_inc(s_evac, 1)
                        wait_count(s_evac, i * 8 + (t0 + j + 1))
                        nc.scalar.activation(relu, relu, ACT.Square).then_inc(s_relu, 1)
                        wait_count(s_relu, i * 8 + (r0 + j + 1))
                        nc.scalar.activation(hidden[:, bass.ds(i * 8 + j, 1), 0, :]
                                             .rearrange("p o t -> p (o t)"), relu, ACT.Copy).then_inc(s_hid, 1)
                seen["tile"] += FF // P
                seen["used"] += FF // P
                seen["relu"] += FF // P
                seen["hid"] += FF // P
                u0 = seen["used"]
                for n in range(FF // P):
                    if n + AHEAD < FF // P:
                        weights_high(n + AHEAD)
                    if n % 4 == 3:
                        m = n // 4
                        act.wait_ge(s_used, u0 + n + 1)
                        b = ps[:, (seen["tile"] + m) % LIN_BANKS, :]
                        nc.scalar.activation(h[:, m, :], b, ACT.Square, scale=1.0 / W_SCALE).then_inc(s_sq, 1)
                        nc.scalar.activation(y[:, m, :], b, ACT.Copy, scale=1.0 / W_SCALE).then_inc(s_evac, 1)
                seen["tile"] += C
                seen["used"] += FF // P
                seen["sq"] += C
                if with_ada:
                    copy(mod[:, :], n=6 * C)
                rms(rinv, D)

            def stick_breaking():
                input_norm(0)
                for m in range(16):
                    copy(arena[:, m, :], 1, scale=SB_D ** -0.5 if m < 8 else 1.0)
                for half in range(2):
                    for tb in range(TB):
                        tokens_copy(arena[:, 20 + 2 * tb + half, :], tb)
                jobs = [(hd, kb) for hd in range(SB_H) for kb in (3, 2, 1, 0)]
                nc.scalar.preload_act_table_set("natural_log_exp_and_others")
                for n in range(len(jobs) + 5):
                    if n < len(jobs):
                        hd, kb = jobs[n]
                        e = arena[:, 28 + kb, 0:T - kb * P]
                        act.wait_ge(s_zc, n + 1)
                        nc.scalar.activation(e, e, ACT.Exp).then_inc(s_ac, 1)
                        seen["ac"] += 1
                        act.wait_ge(s_ac, seen["ac"])
                        nc.scalar.activation(e, e, ACT.Ln, bias=1.0).then_inc(s_sp, 1)
                    if 2 <= n < len(jobs) + 2:
                        hd, kb = jobs[n - 2]
                        if hd >= 2 and kb == 3:
                            act.wait_ge(s_pv, seen["pv"] + hd - 1)
                        act.wait_ge(s_suf, n - 1)
                        w = T - kb * P
                        nc.scalar.activation(y[:, 4 * (hd % 2) + kb, 0:w], ps[:, (n - 2) % 6, 0:w], ACT.Exp)\
                            .then_inc(s_stick, 1)
                    if n >= 8 and n % 4 == 0:
                        hd = n // 4 - 2
                        lo = 64 * (hd % 2)
                        act.wait_ge(s_pv, seen["pv"] + hd + 1)
                        nc.scalar.activation(arena[lo:lo + 64, hd // 2, :], ps[lo:lo + 64, 6 + hd % 2, :],
                                             ACT.Copy).then_inc(s_o, 1)
                seen["pv"] += SB_H
                output()

            def tokens_copy(dst, tb):
                if tb == 0:
                    seen["used"] += 4
                    act.wait_ge(s_used, seen["used"])
                t = seen["tile"]
                seen["tile"] += 1
                nc.scalar.activation(dst, ps[:, t % LIN_BANKS, :], ACT.Copy).then_inc(s_evac, 1)

            def retention():
                input_norm(0)
                trig()
                for hd in range(RET_H):
                    for m in range(4):
                        copy(arena[:, 16 + m, :], 1, scale=1.0 if m < 2 else (D // RET_H) ** -0.5)
                    for tb in range(TB):
                        tokens_copy(arena[:, 20 + tb, :], tb)
                    if hd:
                        act.wait_ge(s_gated, 4 * hd)
                    for m in range(4):
                        copy(arena[:, 24 + m, :], 1, func=ACT.Silu)
                    for m in range(4):
                        seen["pv"] += 1
                        act.wait_ge(s_pv, seen["pv"])
                        b = ps[:, 6 + m % 2, :]
                        square(y[:, 4 + m, :], b)
                        nc.scalar.activation(y[:, m, :], b, ACT.Copy).then_inc(s_o, 1)
                    rms(rinv, 2 * D // RET_H)
                seen["rot"] += 4 * RET_H
                output(2)

            def nsa():
                input_norm(None)
                for m in range(20):
                    copy(arena[:, m, :], 1)
                for m in range(16):
                    copy(arena[:, 28 + m, :], 1, func=ACT.Sigmoid)
                for half in range(2):
                    for tb in range(TB):
                        tokens_copy(arena[:, 20 + 2 * tb + half, :], tb)
                b = tile(1)
                nc.scalar.activation(gates[:, :, :], b.rearrange("p (a n) -> p a n", a=TB)[:, :, 0:24],
                                     ACT.Sigmoid).then_inc(s_evac, 1)
                for kind in range(2):
                    for m in range(2):
                        for g in range(NSA_G):
                            if g == 0:
                                seen["used"] += 4
                                act.wait_ge(s_used, seen["used"])
                            t = seen["tile"]
                            seen["tile"] += 1
                            nc.scalar.activation(cmp_h[:, 4 * kind + 2 * m + g, 0:N_CMP],
                                                 ps[:, t % LIN_BANKS, 0:N_CMP],
                                                 ACT.Gelu_apprx_tanh).then_inc(s_evac, 1)
                copy(cmp_k[:, 0:N_CMP], 0, n=N_CMP)
                b = tile(1)
                nc.scalar.activation(cmp_v[0:N_CMP, :], b[0:N_CMP, 0:P], ACT.Copy).then_inc(s_evac, 1)
                act.wait_ge(s_evac, seen["tile"])
                units = nsa_units()
                for i in range(len(units) + 1):
                    if i < len(units):
                        src, _, n, _, _, _ = units[i]
                        square(tmp[:, 0:n], src)
                        if i:
                            act.wait_ge(s_norm, seen["norm"] + i)
                        rms(rinv, HD, n)
                    if i:
                        n = units[i - 1][2]
                        if i >= 3:
                            act.wait_ge(s_rot, seen["rot"] + i - 2)
                        copy(y[:, i % 2, 0:n], n=n)
                seen["norm"] += len(units)
                seen["rot"] += len(units)
                row_blocks(nsa_rows())
                for m in range(8):
                    copy(y[:, m, :], m % 2)
                for m in range(8):
                    if m >= 4:
                        act.wait_ge(s_merge, m - 3)
                    copy(arena[:, 44 + m % 4, :], int(m % 4 == 3))
                act.wait_ge(s_merge, C)
                for m in range(8):
                    copy(y[:, m, :], 1)

            def experts():
                for k in range(C):
                    if seen["x"]:
                        act.wait_ge(s_x, seen["x"] - C + k + 1)
                    square(h[:, k, :], x[:, k, :])
                rms(rinv, D)
                for k in range(C):
                    act.wait_ge(s_h, seen["h"] + k + 1)
                    nc.scalar.activation(h16[:, k, 0], y[:, k, :], ACT.Copy).then_inc(s_hhigh, 1)
                for m in range(8):
                    copy(arena[:, m, :], 1)
                for tb in range(TB):
                    for four in range(4):
                        b = tile(int(tb == TB - 1 and four == 3))
                        nc.scalar.activation(key_scores[:, tb, 4 * (four // 2):4 * (four // 2) + 4, four % 2, :],
                                             b.rearrange("p (i n) -> p i n", i=4), ACT.Copy).then_inc(s_evac, 1)
                for tb in range(TB):
                    act.wait_ge(s_diff, tb + 1)
                    nc.scalar.activation(exps, exps, ACT.Exp).then_inc(s_gexp, 1)
                    b = tile()
                    now = slice(tb * P, tb * P + P)
                    nc.scalar.activation(chosen[:, 0:2, now], b[:, 0:2 * P].rearrange("p (a n) -> p a n", a=2),
                                         ACT.Copy)
                    nc.scalar.activation(chosen[:, 2, now], b[:, 2 * P:3 * P], ACT.Copy, scale=G_SCALE)
                    nc.scalar.activation(gate32[:, now], b[:, 2 * P:3 * P], ACT.Copy, scale=G_SCALE).then_inc(s_evac, 1)
                for lo, n in PARTS:
                    t0, l0 = seen["tile"], seen["tl"]
                    act.wait_ge(s_w, seen["w"]) if seen["w"] else None
                    with act.Fori(0, T // HOT // 4) as i:
                        for j in range(4):
                            wait_count(s_tile, i * 4 + (l0 + j + 1))
                            dst = part_gates[:, 0:n, bass.ds(i * (4 * HOT) + j * HOT, HOT)]
                            src = ps[:, (t0 + j) % LIN_BANKS, 0:HOT * n].rearrange("p (t e) -> p e t", t=HOT)
                            nc.scalar.activation(dst, src, ACT.Copy, scale=1.0 / G_SCALE).then_inc(s_evac, 1)
                    seen["tile"] += T // HOT
                    seen["tl"] += T // HOT
                    t0, u0, w0 = seen["tile"], seen["used"], seen["w"]
                    last = lo + n == NKEY
                    if lo == 0:
                        for ahead in range(AHEAD):
                            weights_high(ahead)

                    def group(i, final):
                        for j in range(8):
                            weights_high(j + AHEAD, i, 16)
                            if w0 or j >= 2:
                                act.wait_ge(s_w, i * 8 + (w0 + j - 1))
                            elif not isinstance(i, int):
                                act.wait_ge(s_w, i * 8)
                            wait_count(s_used, i * 16 + (u0 + j + 1))
                            nc.scalar.activation((rinv, tmp)[j % 2][:, :], ps[:, (t0 + j) % LIN_BANKS, :],
                                                 ACT.Gelu_apprx_tanh, scale=1.0 / W_SCALE).then_inc(s_evac, 1)
                        for m in range(8):
                            if not (final and m + AHEAD >= 8):
                                weights_high(8 + m + AHEAD, i, 16)

                    with act.Fori(0, n // 8 - int(last)) as i:
                        group(i, False)
                    if last:
                        group(n // 8 - 1, True)
                    seen["tile"] += n
                    seen["used"] += 2 * n
                    seen["w"] += n

            act.wait_ge(s_const, 48)
            act.wait_ge(s_ones, 2)
            if stages[0][1] < LAYERS:
                nc.scalar.activation(cond[:, :], v("c", 0, C), ACT.Silu).then_inc(s_cond, 1)
                copy(mod[:, :], n=6 * C)
            for n, (kind, at) in enumerate(stages):
                if kind == "ffn":
                    ffn(next_layer(at))
                elif kind == "mla":
                    mla()
                elif kind == "sb":
                    stick_breaking()
                elif kind == "ret":
                    retention()
                elif kind == "nsa":
                    nsa()
                else:
                    experts()
                seen["x"] += C
            totals["act"] = seen

        @block.vector
        def _(dve):
            seen = Counter()

            def link(ins):
                seen["vd"] += 1
                ins.then_inc(s_vd, 1)
                dve.wait_ge(s_vd, seen["vd"])

            def tiles(n):
                seen["tile"] += n
                dve.wait_ge(s_evac, seen["tile"])

            def mul(out_, a, b):
                return nc.vector.tensor_tensor(out_, a, b, ALU.mult)

            def add(out_, a, b):
                return nc.vector.tensor_tensor(out_, a, b, ALU.add)

            def scaled(out_, a, factor, b):
                return nc.vector.scalar_tensor_tensor(out=out_, in0=a, scalar=factor, in1=b, op0=ALU.mult,
                                                      op1=ALU.mult)

            def modulation():
                layer = seen["layer"] + stages[0][1]
                tiles(1)
                link(add(mod[:, :], mod[:, :], v("ada_b", 6 * C * layer, 6 * C)))
                for i in range(2):
                    g_in = v("norm_g", (4 * layer + 2 * i) * C, C)
                    g_out = v("norm_g", (4 * layer + 2 * i + 1) * C, C)
                    a = 3 * C * i
                    nc.vector.scalar_tensor_tensor(out=gain[:, 2 * i * C:(2 * i + 1) * C],
                                                   in0=mod[:, a + C:a + 2 * C], scalar=1.0, in1=g_in,
                                                   op0=ALU.add, op1=ALU.mult).then_inc(s_vd, 1)
                    seen["vd"] += 1
                    link(mul(gain[:, (2 * i + 1) * C:(2 * i + 2) * C], mod[:, a + 2 * C:a + 3 * C], g_out))
                seen["layer"] += 1

            def ada_step(g, k, base):
                dve.wait_ge(s_adaw[k % 2], g * (8 * C) + 16 * ((base + k) // 2 + 1))
                dst = ada_sum[:, bass.ds(g * ADA_COLS, ADA_COLS)]
                if k == 0:
                    nc.vector.tensor_scalar(dst, ada_w[:, 0, :], cond[:, 0:1], None, ALU.mult).then_inc(s_adas, 1)
                else:
                    dve.wait_ge(s_adas, g * C + (base + k))
                    nc.vector.scalar_tensor_tensor(out=dst, in0=ada_w[:, k % 2, :], scalar=cond[:, k:k + 1],
                                                   in1=dst, op0=ALU.mult, op1=ALU.add).then_inc(s_adas, 1)

            def ada_accumulate():
                base = seen["ada"]
                with dve.Fori(0, ADA_GROUPS) as g:
                    for k in range(C):
                        ada_step(g, k, base)
                seen["ada"] += ADA_GROUPS * C

            def inverse(buf, n=T):
                link(nc.vector.reciprocal(buf[:, 0:n], buf[:, 0:n]))

            def input_norm(which):
                tiles(1)
                inverse(rinv)
                for k in range(C):
                    g = gain[:, which * C + k:which * C + k + 1] if isinstance(which, int) else v(which, k)
                    scaled(h[:, k, :], x[:, k, :], g, rinv[:, :]).then_inc(
                        s_scaled if isinstance(which, int) else s_h, 1)

            def weights_low(n, loops=0):
                at = seen["used"] + n
                dve.wait_ge(s_whigh, loops + (seen["split"] + n + 1))
                nc.vector.scalar_tensor_tensor(out=halves[:, at % RING, 1, :], in0=ring[:, at % RING, :],
                                               scalar=W_SCALE, in1=halves[:, at % RING, 0, :], op0=ALU.mult,
                                               op1=ALU.subtract).then_inc(s_wlow, 1)

            def split_input(which, ahead):
                tiles(1)
                inverse(rinv)
                for k in range(C):
                    g = gain[:, which * C + k:which * C + k + 1] if isinstance(which, int) else v(which, k)
                    scaled(y[:, k, :], x[:, k, :], g, rinv[:, :]).then_inc(
                        s_scaled if isinstance(which, int) else s_h, 1)
                for k in range(C):
                    dve.wait_ge(s_hhigh, seen["hhigh"] + k + 1)
                    nc.vector.tensor_tensor(h16[:, k, 1], y[:, k, :], h16[:, k, 0], ALU.subtract)\
                        .then_inc(s_hlow, 1)
                    if k < ahead:
                        weights_low(k)
                seen["hhigh"] += C

            def output(which):
                tiles(C + 1)
                inverse(rinv)
                for k in range(C):
                    link(scaled(y[:, k, :], y[:, k, :], gain[:, which * C + k:which * C + k + 1], rinv[:, :]))
                    add(x[:, k, :], x[:, k, :], y[:, k, :]).then_inc(s_x, 1)

            def angles(inv):
                dve.wait_ge(s_phase, seen["phase"])
                link(nc.vector.tensor_copy(y[:, 2, :], pc[:, 6 * T:7 * T].bitcast(i32)))
                link(nc.vector.tensor_scalar(y[:, 0, :], y[:, 2, :], inv, None, ALU.mult))
                for i, turn in enumerate((0.25, 0.0)):
                    k, r = y[:, 1, :], pc[:, i * T:i * T + T]
                    link(nc.vector.tensor_scalar(k, y[:, 0, :], 1.0 / (2 * np.pi), turn, ALU.mult, ALU.add))
                    link(nc.vector.tensor_scalar(k, k, ROUND, None, ALU.add))
                    link(nc.vector.tensor_scalar(k, k, -ROUND, None, ALU.add))
                    src = y[:, 0, :]
                    for part in TWO_PI:
                        link(nc.vector.scalar_tensor_tensor(out=r, in0=k, scalar=-part, in1=src, op0=ALU.mult,
                                                            op1=ALU.add))
                        src = r
                    link(nc.vector.tensor_scalar(r, r, turn * 2 * np.pi, MAX_ANGLE, ALU.add, ALU.min))
                    nc.vector.tensor_scalar(r, r, -MAX_ANGLE, None, ALU.max).then_inc(s_tab, 1)

            def rope(chunk, turned, cos, sin):
                link(mul(turned, turned, sin))
                link(mul(chunk, chunk, cos))
                add(chunk, chunk, turned).then_inc(s_rot, 1)
                seen["rot"] += 1

            def row_blocks(rows):
                base_row, base_pt = seen["row"], seen["pt"]
                done_pt = []
                for i in range(len(rows) + 1):
                    if i < len(rows):
                        r = rows[i]
                        if i >= 2:
                            dve.wait_ge(s_pt, done_pt[i - 2])
                        seen["pt"] += len(r.segs)
                        done_pt.append(seen["pt"])
                        buf = row_buf(h, i).rearrange("p a t -> p (a t)")
                        at = 0
                        for sg in r.segs:
                            g = seen["seg"]
                            dve.wait_ge(s_score, g + 1)
                            nc.vector.tensor_tensor(buf[:, at:at + sg.keys], ps[:, g % 3, 0:sg.keys], sg.mask,
                                                    ALU.add).then_inc(s_masked, 1)
                            seen["seg"] += 1
                            seen["mask"] += 1
                            at += sg.keys
                        dve.wait_ge(s_masked, seen["mask"])
                        nc.vector.tensor_reduce(out=small[:, i % 4:i % 4 + 1], in_=buf[:, 0:at], axis=AX.X,
                                                op=ALU.max, negate=True).then_inc(s_nmax, 1)
                    if i:
                        r = rows[i - 1]
                        keys = sum(sg.keys for sg in r.segs)
                        buf = row_buf(h, i - 1).rearrange("p a t -> p (a t)")[:, 0:keys]
                        total = small[:, 4 + (i - 1) % 4:5 + (i - 1) % 4]
                        inv = small[:, 8 + (i - 1) % 4:9 + (i - 1) % 4]
                        dve.wait_ge(s_prob, base_row + i)
                        link(nc.vector.reciprocal(inv, total))
                        if r.ok is not None:
                            link(mul(inv, inv, r.ok))
                        nc.vector.tensor_scalar(buf, buf, inv, 1.0 if r.gate is None else r.gate, ALU.mult, ALU.mult)\
                            .then_inc(s_normed, 1)
                seen["row"] += len(rows)

            def mla():
                input_norm(0)
                angles(v("inv_mla"))
                tiles(4 + 1)
                inverse(rinv)
                for k in range(2):
                    scaled(arena[:, 29 + k, :], arena[:, 29 + k, :], v("q_norm", 2 * (seen["mla"] // 1) + k),
                           rinv[:, :]).then_inc(s_norm, 1)
                tiles(1)
                inverse(tmp)
                scaled(arena[:, 31, :], arena[:, 31, :], v("kv_norm", seen["mla"]), tmp[:, :]).then_inc(s_norm, 1)
                seen["norm"] += 3
                seen["trig"] += 2
                dve.wait_ge(s_trig, seen["trig"])
                tiles(1)
                rope(arena[:, 28, :], y[:, 3, :], pc[:, 0:T], pc[:, T:2 * T])
                tiles(8 + 8 + 12)
                for m in range(4):
                    tiles(1)
                    rope(arena[:, 8 + m, :], y[:, 4 + m, :], pc[:, 0:T], pc[:, T:2 * T])
                row_blocks(mla_rows())
                output(1)
                seen["mla"] += 1

            def ffn(with_ada):
                split_input(2, AHEAD)
                d0, base = seen["hid"], seen["ada"]
                with dve.Fori(0, FF // P // 8) as i:
                    for j in range(8):
                        weights_low(j + AHEAD, i * 8)
                        if with_ada:
                            ada_step(i, j, base)
                        dve.wait_ge(s_hid, i * 8 + (d0 + j + 1))
                        chunk = hidden[:, bass.ds(i * 8 + j, 1), :, :].rearrange("p o a t -> p (o a) t")
                        nc.vector.tensor_tensor(chunk[:, 1, :], (rinv, tmp)[j % 2][:, :], chunk[:, 0, :],
                                                ALU.subtract).then_inc(s_hidl, 1)
                if with_ada:
                    seen["ada"] += ADA_GROUPS * C
                seen["hid"] += FF // P
                seen["tile"] += FF // P
                seen["used"] += FF // P
                seen["split"] += FF // P
                for n in range(FF // P - AHEAD):
                    weights_low(n + AHEAD)
                seen["used"] += FF // P
                seen["split"] += FF // P
                if with_ada:
                    seen["tile"] += 1
                output(3)
                if with_ada:
                    seen["tile"] -= 1
                    modulation()

            def stick_breaking():
                input_norm(0)
                tiles(16 + 8)
                dve.wait_ge(s_phase, seen["phase"])
                jobs = [(hd, kb) for hd in range(SB_H) for kb in (3, 2, 1, 0)]
                for n in range(len(jobs) + 1):
                    if n < len(jobs):
                        hd, kb = jobs[n]
                        w = T - kb * P
                        dve.wait_ge(s_z, n + 1)
                        nc.vector.tensor_scalar(arena[:, 28 + kb, 0:w], ps[:, n % 6, 0:w], CLAMP, None, ALU.min)\
                            .then_inc(s_zc, 1)
                    if n:
                        hd, kb = jobs[n - 1]
                        w = T - kb * P
                        if hd >= 2 and kb == 3:
                            dve.wait_ge(s_suf, 4 * (hd - 1))
                        dve.wait_ge(s_sp, n)
                        dst, e, z = h[:, 4 * (hd % 2) + kb, :], arena[:, 28 + kb, :], ps[:, (n - 1) % 6, :]
                        link(nc.vector.tensor_tensor(dst[:, 0:w], e[:, 0:w], z[:, 0:w], ALU.max))
                        mul(dst[:, 0:P], dst[:, 0:P], const("sb", "strict")).then_inc(s_log, 1)
                output(1)

            def retention():
                input_norm(0)
                angles(v("inv_ret"))
                seen["trig"] += 2
                dve.wait_ge(s_trig, seen["trig"])
                cos, sin = pc[:, 0:T], pc[:, T:2 * T]
                for hd in range(RET_H):
                    tiles(4)
                    for a in (16, 18):
                        first, second = arena[:, a, :], arena[:, a + 1, :]
                        mul(y[:, 4, :], first, cos).then_inc(s_vd, 1)
                        mul(y[:, 5, :], second, sin).then_inc(s_vd, 1)
                        mul(y[:, 6, :], second, cos).then_inc(s_vd, 1)
                        seen["vd"] += 3
                        link(mul(y[:, 7, :], first, sin))
                        nc.vector.tensor_tensor(first, y[:, 4, :], y[:, 5, :], ALU.subtract).then_inc(s_rot, 1)
                        add(second, y[:, 6, :], y[:, 7, :]).then_inc(s_rot, 1)
                        seen["rot"] += 2
                        dve.wait_ge(s_rot, seen["rot"])
                    decay = const("ret", "decay")[:, hd * T:hd * T + T]
                    for kb in range(TB):
                        w = T - kb * P
                        n = seen["seg"]
                        dve.wait_ge(s_score, n + 1)
                        mul(arena[:, 28 + kb, 0:w], ps[:, 4 + kb % 2, 0:w], decay[:, 0:w]).then_inc(s_dec, 1)
                        seen["seg"] += 1
                    tiles(4 + 4 + 1)
                    inverse(rinv)
                    for m in range(4):
                        link(scaled(y[:, m, :], y[:, m, :], v("gn_g", 4 * hd + m), rinv[:, :]))
                        mul(arena[:, 4 * hd + m, :], y[:, m, :], arena[:, 24 + m, :]).then_inc(s_gated, 1)
                output(1)

            def nsa():
                input_norm("norm1")
                tiles(20)
                dve.wait_ge(s_phase, seen["phase"])
                for kind, name in enumerate(("pe_k", "pe_v")):
                    raw = arena[:, 6 + kind, :].rearrange("p (c s) -> p c s", s=16)
                    for late in range(2):
                        dst = arena[:, 44 + 2 * kind + late, :].rearrange("p (c s) -> p c s", s=16)
                        pos = v(name, 16 * late, 16).rearrange("p (o s) -> p o s", o=1).to_broadcast([P, T // 16, 16])
                        add(dst, raw, pos).then_inc(s_pe, 1)
                for name in ("nsa_q", "dil_q"):
                    link(nc.vector.tensor_scalar(v(name, 0, VEC_WIDTHS[name]), v(name, 0, VEC_WIDTHS[name]),
                                                 HD ** -0.5, None, ALU.mult))
                tiles(16 + 8 + 1 + 8 + 2)
                units = nsa_units()
                for i in range(len(units) + 1):
                    if i < len(units):
                        src, g, n, _, _, _ = units[i]
                        tiles(1)
                        inverse(rinv, n)
                        scaled(src, src, g, rinv[:, 0:n]).then_inc(s_norm, 1)
                        seen["norm"] += 1
                    if i:
                        src, _, n, cos, sin, _ = units[i - 1]
                        tiles(1)
                        dve.wait_ge(s_norm, seen["norm"])
                        rope(src, y[:, i % 2, 0:n], cos, sin)
                row_blocks(nsa_rows())
                seen["tile"] += 8
                for m in range(8):
                    tiles(1)
                    link(mul(y[:, m, :], y[:, m, :], arena[:, 28 + m, :]))
                    link(mul(arena[:, 44 + m % 4, :], arena[:, 44 + m % 4, :], arena[:, 36 + m, :]))
                    add(h[:, m, :], y[:, m, :], arena[:, 44 + m % 4, :]).then_inc(s_merge, 1)
                for m in range(C):
                    tiles(1)
                    add(x[:, m, :], x[:, m, :], y[:, m, :]).then_inc(s_x, 1)

            def each_row(op, count):
                for i in range(count - 1):
                    op(i)
                link(op(count - 1))

            def choose(values, indices, scores, rows):
                for k in (slice(0, 8), slice(8, 16)):
                    each_row(lambda i: nc.vector.max(values(i)[:, k], scores(i)), rows)
                    each_row(lambda i: nc.vector.max_index(indices(i)[:, k], values(i)[:, k], scores(i)), rows)
                    if k.start == 0:
                        each_row(lambda i: nc.vector.match_replace(out=scores(i), in_to_replace=values(i)[:, k],
                                                                   in_values=scores(i), imm_value=LOWEST), rows)

            def experts():
                split_input("norm2", 0)
                seen["tile"] += 8
                seen["used"] = n_slots - 2 * NKEY
                dve.wait_ge(s_phase, seen["phase"])
                iota, iota16 = const("peer", "iota"), const("peer", "iota16")
                wide = [P, PEER_H, PEER_K, PEER_K]
                for tb in range(TB):
                    if tb == 0:
                        tiles(16)
                    else:
                        dve.wait_ge(s_evac, seen["tile"])
                    choose(lambda i: top_v[:, i // 2, i % 2, :], lambda i: top_i[:, i // 2, i % 2, :],
                           lambda i: key_scores[:, tb, i // 2, i % 2, :], 2 * PEER_H)
                    first = top_v[:, :, 0, :].rearrange("p h (k o) -> p h k o", o=1).to_broadcast(wide)
                    second = top_v[:, :, 1, :].rearrange("p h (o k) -> p h o k", o=1).to_broadcast(wide)
                    link(add(cand.rearrange("p h (a b) -> p h a b", a=PEER_K), first, second))
                    choose(lambda i: best_v[:, i * PEER_K:(i + 1) * PEER_K],
                           lambda i: best_i[:, i * PEER_K:(i + 1) * PEER_K], lambda i: cand[:, i, :], PEER_H)
                    best = best_v.rearrange("p (h k) -> p h k", h=PEER_H)
                    e = exps.rearrange("p (h k) -> p h k", h=PEER_H)
                    narrow = [P, PEER_H, PEER_K]
                    nc.vector.tensor_tensor(e, best, best[:, :, 0:1].to_broadcast(narrow), ALU.subtract)\
                        .then_inc(s_diff, 1)
                    link(nc.vector.tensor_copy(top_f, top_i))
                    for i in range(2):
                        if i == 0:
                            link(nc.vector.tensor_scalar(digit_i, best_i, 4, None, ALU.logical_shift_right))
                        else:
                            link(nc.vector.tensor_scalar(digit_i, best_i, PEER_K - 1, None, ALU.bitwise_and))
                        link(nc.vector.tensor_copy(digit_f, digit_i))
                        digit = digit_f.rearrange("p (n o) -> p n o", o=1).to_broadcast([P, P, PEER_K])
                        places = iota16.rearrange("p (o a) -> p o a", o=1).to_broadcast([P, P, PEER_K])
                        flat_match = match.rearrange("p h k a -> p (h k) a")
                        link(nc.vector.tensor_tensor(flat_match, digit, places, ALU.is_equal))
                        keys = top_f[:, :, i, :].rearrange("p h (o a) -> p h o a", o=1).to_broadcast(wide)
                        link(mul(match, match, keys))
                        link(nc.vector.tensor_reduce(out=expert[i], in_=flat_match, axis=AX.X, op=ALU.add))
                    dve.wait_ge(s_gexp, tb + 1)
                    link(nc.vector.tensor_reduce(out=small[:, 0:PEER_H], in_=e, axis=AX.X, op=ALU.add))
                    link(nc.vector.reciprocal(small[:, 8:8 + PEER_H], small[:, 0:PEER_H]))
                    total = small[:, 8:8 + PEER_H].rearrange("p (h o) -> p h o", o=1).to_broadcast(narrow)
                    mul(expert[2].rearrange("p (h k) -> p h k", h=PEER_H), e, total).then_inc(s_top, 1)
                    seen["tile"] += 1
                dve.wait_ge(s_evac, seen["tile"])
                nc.vector.tensor_copy(iota_h, iota).then_inc(s_vd, 1)
                seen["vd"] += 1
                link(nc.vector.tensor_tensor(chosen[:, 3, :], gate32, chosen[:, 2, :], ALU.subtract))
                for lo, n in PARTS:
                    b0, t0 = seen["hot"], seen["tile"]
                    with dve.Fori(0, T // HOT // 4) as i:
                        for j in range(4):
                            dve.wait_ge(s_evac, i * 4 + (t0 + j - 1))
                            at = i * (4 * HOT) + j * HOT
                            def per_token(row, width):
                                return chosen[:, row, bass.ds(at, HOT)].rearrange("p (t o) -> p t o", o=1)\
                                    .to_broadcast([P, HOT, width])

                            def per_key(first, width):
                                return iota_h[:, first:first + width].rearrange("p (o e) -> p o e", o=1)\
                                    .to_broadcast([P, HOT, width])

                            nc.vector.tensor_tensor(hot1[:, j % 2], per_key(0, P), per_token(0, P), ALU.is_equal)
                            same = same2[:, 0:HOT * n].rearrange("p (t e) -> p t e", t=HOT)
                            dve.wait_ge(s_hot, i * 4 + (b0 + j))
                            nc.vector.tensor_tensor(same, per_key(lo, n), per_token(1, n), ALU.is_equal)\
                                .then_inc(s_same, 1)
                            dve.wait_ge(s_same, i * 4 + (b0 + j + 1))
                            for part in range(2):
                                dst = hot2[:, j % 2, part, 0:HOT * n].rearrange("p (t e) -> p t e", t=HOT)
                                last = mul(dst, same, per_token(2 + part, n))
                            last.then_inc(s_hot, 1)
                    seen["hot"] += T // HOT
                    seen["tile"] += T // HOT
                    dve.wait_ge(s_evac, seen["tile"])
                    t0, u0, w0 = seen["tile"], seen["used"], seen["w"]
                    last = lo + n == NKEY
                    if lo == 0:
                        for ahead in range(AHEAD):
                            weights_low(ahead)

                    def group(i, final):
                        for j in range(8):
                            weights_low(j + AHEAD, i * 16)
                            dve.wait_ge(s_evac, i * 8 + (t0 + j + 1))
                            gates_ = part_gates[:, bass.ds(i * 8 + j, 1), :].rearrange("p o t -> p (o t)")
                            dve.wait_ge(s_w, i * 8 + (w0 + j))
                            mul(gated, (rinv, tmp)[j % 2][:, :], gates_).then_inc(s_gate_step, 1)
                            dve.wait_ge(s_gate_step, i * 16 + (2 * (w0 + j) + 1))
                            nc.vector.tensor_copy(y16[:, j, 0], gated).then_inc(s_gate_step, 1)
                            dve.wait_ge(s_gate_step, i * 16 + (2 * (w0 + j) + 2))
                            nc.vector.tensor_tensor(y16[:, j, 1], gated, y16[:, j, 0], ALU.subtract)\
                                .then_inc(s_w, 1)
                        for m in range(C):
                            if not (final and m + AHEAD >= 8):
                                weights_low(8 + m + AHEAD, i * 16)
                            dve.wait_ge(s_used, i * 16 + (u0 + 8 + m + 1))
                            nc.vector.scalar_tensor_tensor(out=x[:, m, :], in0=ps[:, 4 + m % 4, :],
                                                           scalar=1.0 / W_SCALE, in1=x[:, m, :], op0=ALU.mult,
                                                           op1=ALU.add).then_inc(s_x, 1)

                    with dve.Fori(0, n // 8 - int(last)) as i:
                        group(i, False)
                    if last:
                        group(n // 8 - 1, True)
                    seen["split"] += 2 * n
                    seen["w"] += n
                    seen["tile"] += n
                    seen["used"] += 2 * n

            dve.wait_ge(s_const, 48)
            if stages[0][1] < LAYERS:
                dve.wait_ge(s_cond, 1)
                ada_accumulate()
                modulation()
            for n, (kind, at) in enumerate(stages):
                if kind in PHASE_WIDTHS:
                    seen["phase"] += 32 if kind in PHASE_OFFSET else 16
                seen["used"] = sum(slots_of(s) for s in stages[:n])
                if kind == "ffn":
                    ffn(next_layer(at))
                elif kind == "mla":
                    mla()
                elif kind == "sb":
                    stick_breaking()
                elif kind == "ret":
                    retention()
                elif kind == "nsa":
                    nsa()
                else:
                    experts()
            totals["dve"] = seen

        for name in ("tile", "row"):
            assert len({t[name] for e, t in totals.items() if e != "dve" or name == "tile"}) == 1, (name, totals)
        assert totals["pe"]["slot"] == n_slots == totals["act"]["used"], (n_slots, totals)


def x_updates(stages):
    return sum(16 if kind == "peer" else 1 for kind, _ in stages)


ROUND = 1.5 * 2 ** 23
TWO_PI = (6.28125, 0.0019350051879882812, 3.019916050561733e-07)
MAX_ANGLE = 3.1415925
CLAMP = 40.0
LOWEST = -3.0e38
W_SCALE = 256.0
G_SCALE = 1024.0


def tile_slots(tiles):
    n = tiles.shape[0]
    assert n % 8 == 0
    return tiles.reshape(n // 8, 8, P, P).transpose(0, 2, 1, 3).reshape(n // 8, P, SLOT)


def feature_slots(w):
    k, n = w.shape
    return tile_slots(w.reshape(k // P, P, n // P, P).transpose(2, 0, 1, 3).reshape(-1, P, P))


def token_slots(w):
    k, n = w.shape
    return w.reshape(k // 256, 2, P, n // T, T).transpose(3, 0, 2, 1, 4).reshape(-1, P, SLOT)


def pad_tiles(w, tiles):
    out = np.zeros((w.shape[0], tiles * P), w.dtype)
    out[:, :w.shape[1]] = w
    return out


def by_chunk(a):
    return np.ascontiguousarray(np.asarray(a).reshape(-1, P).T)


def stage_slots(stage, a):
    kind, layer = stage
    if kind == "ffn":
        return [feature_slots(a["ffn_w1"][layer]), feature_slots(a["ffn_w2"][layer])]
    if kind == "mla":
        j = layer // 3
        w_in = a["mla_w_in"][j]
        kv = a["mla_w_kv_up"][j].reshape(P, MLA_H, 2, P)
        q = a["mla_w_q_up"][j].reshape(256, MLA_H, MLA_NOPE + MLA_ROPE)
        return [feature_slots(np.concatenate([w_in, w_in[:, 384:448]], 1)),
                kv[:, :, 0].reshape(1, P, SLOT), kv[:, :, 1].reshape(1, P, SLOT),
                feature_slots(np.concatenate([q[:, :, :MLA_NOPE].reshape(256, -1), q[:, :, MLA_NOPE:].reshape(256, -1)], 1)),
                feature_slots(a["mla_w_out"][j])]
    if kind == "sb":
        w = a["sb_w_in"][0]
        return [feature_slots(w[:, :2 * D]), token_slots(w[:, 2 * D:]), feature_slots(a["sb_w_out"][0])]
    if kind == "ret":
        w = a["ret_w_in"][0]
        out = []
        for hd in range(RET_H):
            k = slice(256 * hd, 256 * hd + 256)
            vv = slice(512 * hd, 512 * hd + 512)
            out += [feature_slots(np.concatenate([w[:, 0:D][:, k], w[:, D:2 * D][:, k]], 1)),
                    token_slots(w[:, 2 * D:4 * D][:, vv]), feature_slots(w[:, 4 * D:6 * D][:, vv])]
        return out + [feature_slots(a["ret_w_out"][0])]
    if kind == "nsa":
        w = a["w_in_2"]
        q, kc, vc, ks, vs, kw, vw, g, dil, mg = np.split(w, np.cumsum([512] + [128] * 6 + [24, 2304]), axis=1)
        q = q.reshape(D, NSA_G, 4, HD).transpose(0, 2, 1, 3).reshape(D, 512)
        dil = dil.reshape(D, DIL_G, 3, 256)
        out = [feature_slots(np.concatenate([q, ks, kw, kc, vc, dil[:, :, 0:2].reshape(D, -1), mg], 1)),
               token_slots(np.concatenate([vs, vw, dil[:, :, 2].reshape(D, -1)], 1)), feature_slots(pad_tiles(g, 1))]
        for name in ("k", "v"):
            w1 = a[f"cmp_w1_{name}_2"].reshape(32, HD, 2, P).transpose(2, 0, 1, 3).reshape(64, HD, P)
            out.append(tile_slots(np.concatenate([w1, w1], 1)))
        w2 = np.concatenate([a[f"cmp_w2_{name}_2"].reshape(2, P, HD)[m] for name in ("k", "v") for m in range(2)], 1)
        out.append(pad_tiles(w2, 8)[None])
        up = a["w_up_nsa_2"].reshape(NSA_G, 4, HD, D).transpose(1, 0, 2, 3).reshape(512, D)
        return out + [feature_slots(up), feature_slots(a["w_up_dil_2"]), feature_slots(a["w_o_2"])]
    sub = a["peer_subkeys_2"].transpose(0, 2, 1).reshape(P, NKEY)
    u = a["peer_u_2"].reshape(NKEY, 16, 8, C, P).transpose(1, 2, 4, 3, 0).reshape(16, 8, P, SLOT)
    vv = a["peer_v_2"].reshape(NKEY, 16, 8, C, P).transpose(1, 3, 0, 2, 4).reshape(16, 8, P, SLOT)
    return [feature_slots(a["peer_wq_2"]), pad_tiles(sub, 8)[None],
            np.concatenate([u, vv], 1).reshape(-1, P, SLOT)]


def vectors(a):
    def twice(g):
        g = np.asarray(g).reshape(-1, HD)
        return np.concatenate([g, g], 1).T
    inv = lambda n, dim: (np.float32(10000.0) ** (-np.arange(0, dim, 2, dtype=np.float32) / np.float32(dim)))
    parts = {
        "c": by_chunk(a["c"]), "norm_g": by_chunk(a["norm_g"]), "ada_b": by_chunk(a["ada_b"]),
        "q_norm": by_chunk(a["mla_q_norm"]), "kv_norm": by_chunk(a["mla_kv_norm"]), "gn_g": by_chunk(a["ret_gn_g"]),
        "norm1": by_chunk(a["norm1_g_2"]), "norm2": by_chunk(a["norm2_g_2"]), "nsa_q": twice(a["nsa_q_norm_2"]),
        "nsa_k": twice(a["nsa_k_norm_2"]), "dil_q": twice(a["dil_q_norm_2"]), "dil_k": twice(a["dil_k_norm_2"]),
        "pe_k": twice(a["cmp_pe_k_2"]), "pe_v": twice(a["cmp_pe_v_2"]),
        "inv_mla": np.tile(inv(0, MLA_ROPE), 4)[:, None], "inv_ret": inv(0, D // RET_H)[:, None],
        "row_ok": (np.arange(P) >= 31).astype(np.float32)[:, None],
    }
    assert {k: p.shape for k, p in parts.items()} == {k: (P, w) for k, w in VEC_WIDTHS.items()}
    return np.concatenate([parts[k] for k in VEC_WIDTHS], 1).astype(np.float32)


def turn_matrix(size, half):
    m = np.zeros((P, P), np.float32)
    for base in range(0, P, size):
        for i in range(half):
            m[base + i + half, base + i] = -1.0
            m[base + i, base + i + half] = 1.0
    return m


def constant_matrices():
    pair = np.kron(np.eye(2), np.ones((HD, HD)))
    return np.stack([np.eye(P), turn_matrix(64, 32), turn_matrix(HD, 8), pair], 1).astype(np.float32)


def phase_constants(kind):
    p = np.arange(P)[:, None]
    rel = p + (TB - 1) * P - np.arange(T)[None, :]
    if kind == "mla":
        parts = {"causal": np.where(rel >= 0, 0.0, NEG)}
    elif kind == "sb":
        k, q = np.arange(P)[:, None], np.arange(P)[None, :]
        parts = {"strict": k < q, "fill_future": np.where(k < q, 0.0, NEG), "suffix": -1.0 * (k >= q),
                 "minus_ones": -np.ones((P, P))}
    elif kind == "ret":
        log_gamma = np.log(1.0 - 2.0 ** (-5.0 - np.arange(RET_H)))
        d = np.arange(T)[None, :] - p
        parts = {"decay": np.concatenate([np.where(d >= 0, np.exp(np.maximum(d, 0) * g), 0.0) for g in log_gamma], 1)}
    elif kind == "nsa":
        inv = np.float32(500000.0) ** (-(np.arange(8, dtype=np.float32) * 2.0 / 16)).astype(np.float32)
        ang = (np.arange(T, dtype=np.float32)[None, :] * inv[:, None]).astype(np.float64)
        cos, sin = np.ones((HD, T)), np.zeros((HD, T))
        cos[:16], sin[:16] = np.tile(np.cos(ang), (2, 1)), np.tile(np.sin(ang), (2, 1))
        ends = np.arange(32) * 16 + 31
        t = p + P * np.arange(TB)[None, :]
        parts = {"cos": np.tile(cos, (2, 1)), "sin": np.tile(sin, (2, 1)), "causal": np.where(rel >= 0, 0.0, NEG)}
        for i, dil in enumerate(DILATIONS):
            ok = (rel >= 0) & (rel % dil == 0) & (rel // dil <= P)
            parts[f"dil{i}"] = np.where(ok, 0.0, NEG)
        parts["cmp_mask"] = np.where(ends[None, None, :] <= t[:, :, None], 0.0, NEG).reshape(P, -1)
    else:
        parts = {"iota": np.tile(np.arange(P), (P, 1)), "iota16": np.tile(np.arange(PEER_K), (P, 1))}
    assert {k: v.shape[1] for k, v in parts.items()} == PHASE_WIDTHS[kind]
    return np.concatenate([parts[k] for k in PHASE_WIDTHS[kind]], 1).astype(np.float32)


def arrays_of(a, stages):
    weights = np.concatenate([w for s in stages for w in stage_slots(s, a)], 0)
    first = stages[0][1]
    out = {
        "wstream": weights,
        "vecs": vectors(a), "mats": constant_matrices(),
        "x_in": np.ascontiguousarray(a["x"][0].T.reshape(C, P, T).transpose(1, 0, 2)),
        "positions": np.asarray(a["positions"], np.int32).reshape(1, T),
        "ada": np.ascontiguousarray(a["ada_w"][first:].reshape(-1, C, P, ADA_GROUPS, ADA_COLS)
                                    .transpose(0, 3, 1, 2, 4).reshape(-1, P, ADA_COLS)) if first < LAYERS
        else np.zeros((1, P, ADA_COLS), np.float32),
    }
    for kind in PHASE_WIDTHS:
        out[f"phase_{kind}"] = phase_constants(kind)
    return out


def program(nc, arrays, stages):
    aps = {k: nc.dram_tensor(k, v.shape, mybir.dt.from_np(v.dtype), kind="ExternalInput").ap()
           for k, v in arrays.items()}
    out = nc.dram_tensor("out", (P, C, T), mybir.dt.float32, kind="ExternalOutput").ap()
    build(nc, aps["wstream"], aps["ada"], aps["vecs"], aps["mats"],
          {k: aps[f"phase_{k}"] for k in PHASE_WIDTHS}, aps["x_in"], aps["positions"], out, stages)


def kernel(**inputs):
    import concourse.bacc as bacc
    from concourse.bass_utils import run_bass_kernel_spmd

    a = {k: np.asarray(v) for k, v in inputs.items()}
    arrays = arrays_of(a, STAGES)
    nc = bacc.Bacc("TRN2", target_bir_lowering=False, num_devices=1)
    program(nc, arrays, STAGES)
    result = run_bass_kernel_spmd(nc, [arrays], core_ids=[0])
    return result.results[0]["out"].transpose(2, 1, 0).reshape(1, T, D)
```
